# Optimizing a Trainium2 kernel written in Bass

```python
import jax, jax.numpy as jnp
from jax import lax
import numpy as np

D_MODEL = 2048
BATCH = 1
SEQ = 256
DEPTH = 1

CHUNK = 64
N_META = 16
ATT_HEADS = 16
ATT_HEAD_DIM = 128
ATT_WIDTH = ATT_HEADS * ATT_HEAD_DIM
CONV_WIDTH = D_MODEL
CONV_GROUPS = 16
CONV_K = 3
Q_BLOCK = 128
EPS = 1e-6
_IN_SIZES = (ATT_WIDTH, ATT_WIDTH, ATT_WIDTH, ATT_HEADS, ATT_WIDTH,
             CONV_WIDTH, CONV_WIDTH, CONV_WIDTH, CONV_WIDTH, D_MODEL, D_MODEL)
N_IN = 4 * ATT_WIDTH + ATT_HEADS + 4 * CONV_WIDTH + 2 * D_MODEL

kernel_name = "fox_shortconv_gated_hybrid_block"

def _split_points():
    pts, acc = [], 0
    for s in _IN_SIZES[:-1]:
        acc += s
        pts.append(acc)
    return pts

def rmsnorm(x, g):
    xf = x.astype(jnp.float32)
    y = xf * lax.rsqrt(jnp.mean(xf * xf, axis=-1, keepdims=True) + EPS)
    return (y * g.astype(jnp.float32)).astype(x.dtype)

def forgetting_attention(q, k, v, log_f):
    b, l, h, dh = q.shape
    nb = l // Q_BLOCK
    c = jnp.cumsum(log_f, axis=1).transpose(0, 2, 1)
    scale = dh ** -0.5
    kpos = jnp.arange(l)
    q_blocks = q.reshape(b, nb, Q_BLOCK, h, dh).transpose(1, 0, 3, 2, 4)
    c_blocks = c.reshape(b, h, nb, Q_BLOCK).transpose(2, 0, 1, 3)
    starts = jnp.arange(nb) * Q_BLOCK

    def one_block(args):
        q_blk, c_blk, start = args
        s = jnp.einsum('bhqd,bkhd->bhqk', q_blk, k).astype(jnp.float32) * scale
        s = s + (c_blk[..., None] - c[:, :, None, :])
        qpos = start + jnp.arange(Q_BLOCK)
        causal = kpos[None, :] <= qpos[:, None]
        p = jax.nn.softmax(jnp.where(causal, s, -jnp.inf), axis=-1)
        return jnp.einsum('bhqk,bkhd->bqhd', p.astype(v.dtype), v)

    out = lax.map(one_block, (q_blocks, c_blocks, starts))
    return out.transpose(1, 0, 2, 3, 4).reshape(b, l, h * dh)

def short_conv(u, w):
    l = u.shape[1]
    up = jnp.pad(u, ((0, 0), (CONV_K - 1, 0), (0, 0)))
    out = up[:, 0:l] * w[0]
    for j in range(1, CONV_K):
        out = out + up[:, j:j + l] * w[j]
    return out

def hybrid_layer(x, norm_g, w_in, b_f, conv_w, w_att_o, w_conv_o, w_out):
    b, l, _ = x.shape
    h = rmsnorm(x, norm_g)
    proj = jnp.einsum('bld,dn->bln', h, w_in)
    (q, k, v, f_logit, z_att, u, gate_b, gate_c, z_conv,
     m_att, m_conv) = jnp.split(proj, _split_points(), axis=-1)
    heads = lambda t: t.reshape(b, l, ATT_HEADS, ATT_HEAD_DIM)
    log_f = jax.nn.log_sigmoid((f_logit + b_f).astype(jnp.float32))
    o_att = forgetting_attention(heads(q), heads(k), heads(v), log_f)
    y_att = jnp.einsum('blc,cd->bld', o_att * jax.nn.silu(z_att), w_att_o)
    o_conv = gate_b * short_conv(gate_c * u, conv_w)
    y_conv = jnp.einsum('blc,cd->bld', o_conv * jax.nn.silu(z_conv), w_conv_o)
    merged = jax.nn.sigmoid(m_att) * y_att + jax.nn.sigmoid(m_conv) * y_conv
    return x + jnp.einsum('bld,de->ble', merged, w_out)

def setup_inputs(seed: int = 0) -> dict:
    key = jax.random.key(seed)
    ks = jax.random.split(key, 11)
    f32 = jnp.float32
    x = jax.random.normal(ks[0], (BATCH, SEQ, D_MODEL), f32)
    meta_tokens = jax.random.normal(ks[1], (N_META, D_MODEL), f32)
    norm_gain = 1.0 + 0.01 * jax.random.normal(ks[2], (DEPTH, D_MODEL), f32)
    w_in = jax.random.normal(ks[3], (DEPTH, D_MODEL, N_IN), f32) * D_MODEL ** -0.5
    b_f = (jnp.linspace(1.0, 6.0, ATT_HEADS, dtype=f32)[None, :]
           + 0.1 * jax.random.normal(ks[4], (DEPTH, ATT_HEADS), f32))
    conv_w = jax.random.normal(ks[5], (DEPTH, CONV_K, CONV_WIDTH), f32) * CONV_K ** -0.5
    w_att_o = jax.random.normal(ks[6], (DEPTH, ATT_WIDTH, D_MODEL), f32) * ATT_WIDTH ** -0.5
    w_conv_o = jax.random.normal(ks[7], (DEPTH, CONV_WIDTH, D_MODEL), f32) * CONV_WIDTH ** -0.5
    w_out = jax.random.normal(ks[8], (DEPTH, D_MODEL, D_MODEL), f32) * D_MODEL ** -0.5
    final_gain = 1.0 + 0.01 * jax.random.normal(ks[9], (D_MODEL,), f32)
    return {"x": x, "meta_tokens": meta_tokens, "norm_gain": norm_gain, "w_in": w_in,
            "b_f": b_f, "conv_w": conv_w, "w_att_o": w_att_o, "w_conv_o": w_conv_o,
            "w_out": w_out, "final_gain": final_gain}

def reference(x, meta_tokens, norm_gain, w_in, b_f, conv_w, w_att_o, w_conv_o, w_out, final_gain):
    b = x.shape[0]
    l_real = N_META + x.shape[1]
    l_pad = -(-l_real // Q_BLOCK) * Q_BLOCK
    meta = jnp.broadcast_to(meta_tokens.astype(x.dtype)[None], (b, N_META, D_MODEL))
    hdn = jnp.concatenate([meta, x], axis=1)
    hdn = jnp.pad(hdn, ((0, 0), (0, l_pad - l_real), (0, 0)))
    for i in range(DEPTH):
        hdn = hybrid_layer(hdn, norm_gain[i], w_in[i], b_f[i], conv_w[i],
                           w_att_o[i], w_conv_o[i], w_out[i])
    hdn = rmsnorm(hdn, final_gain)
    return hdn[:, N_META:l_real]


_drawn_inputs = setup_inputs


def setup_inputs(seed=0):
    import zlib

    import numpy as np

    out = dict(_drawn_inputs(seed))
    spreads = {}
    factors = {}
    for name, (base, spread) in spreads.items():
        noise = np.random.default_rng([zlib.crc32(name.encode()), seed]).standard_normal(out[name].shape)
        drawn = base * np.exp(spread * noise) if base else spread * noise
        out[name] = __import__('jax').numpy.asarray(drawn.astype(out[name].dtype))
    for name, factor in factors.items():
        out[name] = (out[name] * factor).astype(out[name].dtype)
    return out
```

```python
from contextlib import ExitStack

import concourse.bass as bass
from concourse import mybir

F32 = mybir.dt.float32
F32R = mybir.dt.float32r
ALU = mybir.AluOpType
ACT = mybir.ActivationFunctionType
AX = mybir.AxisListType

P = 128
D = 2048
SEQ = 256
META = 16
TOK = META + SEQ
HEADS = 16
DH = 128
TAPS = 3
EPS = 1e-6
SCALE = DH ** -0.5
NEG = -1e30

KT = D // P
PAIRS = KT // 2
CONV_TOK = SEQ + TAPS - 1

COL_Q, COL_K, COL_V, COL_F = 0, D, 2 * D, 3 * D
COL_Z = COL_F + HEADS
COL_U, COL_GB, COL_GC, COL_ZC = COL_Z + D, COL_Z + 2 * D, COL_Z + 3 * D, COL_Z + 4 * D
COL_MA, COL_MC = COL_Z + 5 * D, COL_Z + 6 * D

UNIT = 1024
RAW, RING, LEAD = 4, 8, 5
UK = 4
PER = KT // UK
N_CONV, N_F, N_MERGE, N_ATT, N_OUT = 4 * PER, 2, 2 * PER, 4 * PER, 2 * KT
U_CONV = 0
U_F = U_CONV + N_CONV * PAIRS
U_MC = U_F + N_F
U_ATT = U_MC + N_MERGE * PAIRS
U_MA = U_ATT + N_ATT * PAIRS
U_OUT = U_MA + N_MERGE * PAIRS
UNITS = U_OUT + N_OUT
OUT_STEP = 8
OUT_K = OUT_STEP // 2

K0 = META + P
SC = K0 + TOK

OUT_BANK = (4, 0)
A, B, C, E = 0, 2, 4, 6
FREE_A = {"conv": 1, "mc": 1 + PAIRS, "att": 1 + 2 * PAIRS, "ma": 1 + 4 * PAIRS, "out": 1 + 5 * PAIRS}
FREE_B = FREE_A
FREE_C = {"conv": 1, "f": 1 + PAIRS, "att": 2 + PAIRS, "out": 2 + 3 * PAIRS}
FREE_E = {"conv": 1, "att": 1 + PAIRS, "out": 1 + 3 * PAIRS}


def hybrid_block(nc, x, meta_tokens, norm_gain, w_in, b_f, conv_w, w_att_o, w_conv_o, w_out,
                 final_gain, neg_c_dram, out):
    at = {}
    base = (nc.sbuf_base + 31) // 32 * 32

    def region(name, size):
        nonlocal base
        at[name] = base
        base += size

    region("h", 2 * KT * TOK * 4)
    region("o", 2 * KT * SEQ * 4)
    region("p", KT * SEQ * 4)
    region("m", 2 * KT * SEQ * 4)
    region("raw", RAW * UNIT * 4)
    region("hi", RING * UNIT * 4)
    region("lo", RING * UNIT * 4)
    region("misc", 13 * 1024)

    def place(reg, name, shape, dtype=F32):
        t = nc.alloc_sbuf_tensor_at(name, shape, dtype, offset=at[reg])
        size = 4
        for s in shape[1:]:
            size *= s
        at[reg] += (size + 31) // 32 * 32
        return t

    misc = lambda name, shape, dtype=F32: place("misc", name, shape, dtype)
    ident = misc("ident", [P, P])
    chan_rows = misc("chan_rows", [(TAPS + 1) * KT, P])
    chan = misc("chan", [P, TAPS + 1, KT])
    bf = misc("bf", [HEADS, 1])
    mask = misc("mask", [P, SC])
    gate = misc("gate", [P, 2, SEQ])
    prod = misc("prod", [P, 2, SEQ])
    prod2 = misc("prod2", [P, 2, SEQ])
    sumsq = misc("sumsq", [P, 4])
    var = misc("var", [P, 4])
    minus_half = misc("minus_half", [P, 4])
    rstd = misc("rstd", [P, 4])
    nmax = misc("nmax", [P, 2, 2])
    smax = misc("smax", [P, 2, 2])
    den = misc("den", [P, 2, 2])
    rden = misc("rden", [P, 2, 2])

    w_raw = place("raw", "w_raw", [P, RAW, UNIT])
    w_hi = place("hi", "w_hi", [P, RING, UNIT], F32R)
    w_lo = place("lo", "w_lo", [P, RING, UNIT], F32R)

    h_at, o_at, m_at = at["h"], at["o"], at["m"]
    x_nat = place("o", "x_nat", [P, 2, D])
    meta_nat = place("o", "meta_nat", [META, D])
    square0 = place("o", "square0", [P, D])
    square1 = place("m", "square1", [P, D])
    at["o"], at["m"] = o_at, m_at
    h_hi = place("h", "h_hi", [P, KT, TOK], F32R)
    h_lo = place("h", "h_lo", [P, KT, TOK], F32R)
    o_hi = place("o", "o_hi", [P, KT, SEQ], F32R)
    o_lo = place("o", "o_lo", [P, KT, SEQ], F32R)
    p_at = at["p"]
    square_meta = place("p", "square_meta", [META, D])
    at["p"] = p_at
    partial = place("p", "partial", [P, KT, SEQ])
    u_sb = place("m", "u_sb", [P, 2, CONV_TOK])
    cu = place("m", "cu", [P, 2, CONV_TOK])
    conv = [place("m", f"conv{j}", [P, 2, SEQ]) for j in range(TAPS)]
    conv_gated = place("m", "conv_gated", [P, 2, SEQ])
    at["m"] = m_at
    f_x = place("m", "f_x", [HEADS, TOK])
    f_na = place("m", "f_na", [HEADS, TOK])
    f_e = place("m", "f_e", [HEADS, TOK])
    f_l = place("m", "f_l", [HEADS, TOK])
    f_mn = place("m", "f_mn", [HEADS, TOK])
    f_nlog = place("m", "f_nlog", [HEADS, TOK])
    f_one = place("m", "f_one", [HEADS, TOK])
    neg_c = place("m", "neg_c", [HEADS, TOK])
    at["m"] = m_at
    neg_cb = place("m", "neg_cb", [P, 2, TOK])
    bias = place("m", "bias", [P, 2, SC])
    k_t = place("m", "k_t", [P, 2, TOK])
    q_t = place("m", "q_t", [P, 2, SEQ])
    v_t = place("m", "v_t", [P, 2, TOK])
    v_nat = place("m", "v_nat", [P, 2, 3 * P])
    probs = place("m", "probs", [P, 2, SC])
    p_t = place("m", "p_t", [P, 2, 3 * P])
    p_tail = place("m", "p_tail", [META, 2, 2 * META])
    at["m"] = m_at
    m_hi = place("m", "m_hi", [P, KT, SEQ], F32R)
    m_lo = place("m", "m_lo", [P, KT, SEQ], F32R)
    at["h"], at["o"] = h_at, o_at
    x_res = place("h", "x_res", [P, 2, D])
    gain_b = place("h", "gain_b", [P, D])
    y = place("o", "y", [P, 2, D])
    square2 = place("o", "square2", [P, 2, D])

    with ExitStack() as ctx:
        ps = ctx.enter_context(nc.psum_tensor("ps", [P, 8, 512], F32))
        sem = lambda name: ctx.enter_context(nc.semaphore(name))

        x_landed = [sem(f"x_landed{t}") for t in range(3)]
        rows_landed = sem("rows_landed")
        bf_landed = sem("bf_landed")
        w_landed = [sem(f"w_landed{s}") for s in range(RAW)]
        w_rounded = sem("w_rounded")
        w_split = sem("w_split")
        w_used = sem("w_used")
        free = {A: sem("free_a"), B: sem("free_b"), C: sem("free_c"), E: sem("free_e")}
        consts = sem("consts")
        ones_made = sem("ones_made")
        ss_act, ss_dve = sem("ss_act"), sem("ss_dve")
        var_done, rstd_done = sem("var_done"), sem("rstd_done")
        normed = [sem(f"normed{t}") for t in range(3)]
        chan_t, chan_done = sem("chan_t"), sem("chan_done")
        h_turned, h_rounded, h_split = sem("h_turned"), sem("h_rounded"), sem("h_split")
        conv_step, conv_sig = sem("conv_step"), sem("conv_sig")
        o_rounded, o_split = sem("o_rounded"), sem("o_split")
        f_dve, f_act, c_stored = sem("f_dve"), sem("f_act"), sem("c_stored")
        bias_landed, bias_made = sem("bias_landed"), sem("bias_made")
        s_done, exp_done, v_turned, p_turned, pv_done = (
            sem("s_done"), sem("exp_done"), sem("v_turned"), sem("p_turned"), sem("pv_done"))
        att_step, z_exp = sem("att_step"), sem("z_exp")
        merge_step, m_rounded, m_split = sem("merge_step"), sem("m_rounded"), sem("m_split")
        y_tile = sem("y_tile")
        x_res_landed, gain_landed = sem("x_res_landed"), sem("gain_landed")
        y_added, y_ss, y_var, y_rstd, y_scaled = (
            sem("y_added"), sem("y_ss"), sem("y_var"), sem("y_rstd"), sem("y_scaled"))
        stored = sem("stored")

        block = ctx.enter_context(nc.Block())

        CONV_STEPS = 4
        ATT_STEPS = 6

        def count(i, per, c):
            return c if i is None else i * per + c

        @block.sync
        def _(sp):
            def load(i, per, c, src, k=UK):
                sp.wait_ge(w_split, count(i, per, c + 1))
                dst = w_raw[:, c % RAW, :].rearrange("p (k n) -> p k n", k=k)
                sp.dma_start(dst, src).then_inc(w_landed[c % RAW], 16)

            def load_stage(first, sources):
                per = PER * len(sources)
                with sp.Fori(1, PAIRS + 1) as i:
                    for j in range(per):
                        w_k, col = sources[j // PER]
                        rows = slice(j % PER * UK, j % PER * UK + UK)
                        load(i, per, first + j - per,
                             w_k[:, rows, bass.ds(i * (2 * P) + (col - 2 * P), 2 * P)])

            w_in_k, w_conv_k, w_att_k, w_out_k = (
                w.rearrange("(k p) n -> p k n", p=P) for w in (w_in, w_conv_o, w_att_o, w_out))
            for t in range(2):
                sp.dma_start(x_nat[:, t, :], x[t * P:(t + 1) * P, :]).then_inc(x_landed[t], 16)
            sp.dma_start(meta_nat[:], meta_tokens).then_inc(x_landed[2], 16)
            load_stage(U_CONV, [(w_in_k, COL_U), (w_in_k, COL_GC), (w_in_k, COL_GB), (w_in_k, COL_ZC)])
            for j in range(N_F):
                load(None, 0, U_F + j, w_in_k[:, j * 8:j * 8 + 8, COL_F:COL_F + P], k=8)
            load_stage(U_MC, [(w_in_k, COL_MC), (w_conv_k, 0)])
            load_stage(U_ATT, [(w_in_k, COL_K), (w_in_k, COL_Q), (w_in_k, COL_V), (w_in_k, COL_Z)])
            load_stage(U_MA, [(w_in_k, COL_MA), (w_att_k, 0)])
            with sp.Fori(0, N_OUT // OUT_STEP) as i:
                for j in range(OUT_STEP):
                    half = slice(j % 2 * UNIT, (j % 2 + 1) * UNIT)
                    load(i, OUT_STEP, U_OUT + j, w_out_k[:, bass.ds(i * OUT_K + j // 2, 1), half], k=1)
            sp.wait_ge(w_used, RING + U_OUT)
            sp.dma_start(x_res[:], x.rearrange("(t p) d -> p t d", p=P)).then_inc(x_res_landed, 16)
            sp.dma_start(gain_b[:], final_gain.partition_broadcast(P)).then_inc(gain_landed, 16)
            for t in range(2):
                for c in range(2):
                    sp.wait_ge(y_scaled, 2 * t + c + 1)
                    cols = slice(c * UNIT, (c + 1) * UNIT)
                    sp.dma_start(out[t * P:(t + 1) * P, cols], y[:, t, cols]).then_inc(stored, 16)
            sp.wait_ge(stored, 4 * 16)

        @block.gpsimd
        def _(pool):
            nc.gpsimd.memset(ident[:], 1.0).then_inc(ones_made, 1)
            nc.gpsimd.memset(mask[:], 0.0).then_inc(ones_made, 1)
            nc.gpsimd.memset(minus_half[:], -0.5).then_inc(ones_made, 1)
            pool.wait_ge(ones_made, 3)
            nc.gpsimd.affine_select(out=ident[:], in_=ident[:], pattern=[[-1, P]], compare_op=ALU.is_equal,
                                    fill=0.0, base=0, channel_multiplier=1).then_inc(consts, 1)
            nc.gpsimd.affine_select(out=mask[:, 0:K0], in_=mask[:, 0:K0], pattern=[[-1, K0]],
                                    compare_op=ALU.is_ge, fill=NEG, base=META, channel_multiplier=1)
            nc.gpsimd.affine_select(out=mask[:, K0:SC], in_=mask[:, K0:SC], pattern=[[-1, TOK]],
                                    compare_op=ALU.is_ge, fill=NEG, base=K0, channel_multiplier=1
                                    ).then_inc(consts, 1)
            pool.wait_ge(var_done, 2)
            nc.gpsimd.tensor_tensor(rstd[:, 0:2], var[:, 0:2], minus_half[:, 0:2], ALU.pow).then_inc(rstd_done, 1)
            nc.gpsimd.tensor_tensor(rstd[0:META, 2:3], var[0:META, 2:3], minus_half[0:META, 2:3],
                                    ALU.pow).then_inc(rstd_done, 1)
            pool.wait_ge(consts, 2)
            pool.sem_inc(bias_made, 1)
            with pool.Fori(0, PAIRS) as i:
                pool.wait_ge(bias_landed, i * 16 + 16)
                pool.wait_ge(free[C], i * 2 + FREE_C["att"])
                for b in range(2):
                    nc.gpsimd.tensor_tensor(bias[:, b, 0:K0], mask[:, 0:K0], neg_cb[:, b, 0:K0], ALU.add)
                    last = nc.gpsimd.tensor_tensor(bias[:, b, K0:SC], mask[:, K0:SC], neg_cb[:, b, :], ALU.add)
                last.then_inc(bias_made, 1)
            for t in range(2):
                pool.wait_ge(y_var, t + 1)
                nc.gpsimd.tensor_tensor(rstd[:, t:t + 1], var[:, t:t + 1], minus_half[:, t:t + 1],
                                        ALU.pow).then_inc(y_rstd, 1)

        @block.scalar
        def _(act):
            def round_unit(i, per, c):
                act.wait_ge(w_landed[c % RAW], count(i, per // RAW * 16, c // RAW * 16 + 16))
                act.wait_ge(w_used, count(i, per, c + 1))
                nc.scalar.copy(w_hi[:, c % RING, :], w_raw[:, c % RAW, :]).then_inc(w_rounded, 1)

            act.dma_start(chan_rows[0:TAPS * KT, :], conv_w.rearrange("t (k p) -> (t k) p", p=P)).then_inc(rows_landed, 16)
            act.dma_start(chan_rows[TAPS * KT:(TAPS + 1) * KT, :], norm_gain.rearrange("a (k p) -> (a k) p", p=P)).then_inc(rows_landed, 16)
            act.dma_start(bf[:], b_f.rearrange("a h -> h a")).then_inc(bf_landed, 16)

            act.wait_ge(x_landed[0], 16)
            nc.scalar.activation(square0[:], x_nat[:, 0, :], ACT.Square, accum_out=sumsq[:, 0:1]).then_inc(ss_act, 1)
            act.wait_ge(x_landed[2], 16)
            nc.scalar.activation(square_meta[:], meta_nat[:], ACT.Square,
                                 accum_out=sumsq[0:META, 2:3]).then_inc(ss_act, 1)
            round_unit(None, 0, 0)
            act.wait_ge(rstd_done, 1)
            nc.scalar.activation(x_nat[:, 0, :], x_nat[:, 0, :], ACT.Copy, scale=rstd[:, 0:1]).then_inc(normed[0], 1)
            round_unit(None, 0, 1)
            act.wait_ge(chan_done, 1)
            for k in range(KT):
                act.wait_ge(h_turned, k + 1)
                nc.scalar.activation(h_hi[:, k, :], ps[:, k % 8, 0:TOK], ACT.Copy,
                                     scale=chan[:, TAPS, k:k + 1]).then_inc(h_rounded, 1)
                if k % 4 == 3:
                    round_unit(None, 0, 2 + k // 4)

            with act.Fori(0, PAIRS) as i:
                for j in range(1, N_CONV + 1):
                    round_unit(i, N_CONV, U_CONV + j + LEAD)
                    if j == PER:
                        act.wait_ge(w_used, count(i, N_CONV, RING + U_CONV + j))
                        nc.scalar.copy(u_sb[:], ps[:, A:A + 2, 0:CONV_TOK]).then_inc(free[A], 1)
                act.wait_ge(w_used, count(i, N_CONV, RING + U_CONV + N_CONV))
                nc.scalar.activation(gate[:], ps[:, E:E + 2, 0:SEQ], ACT.Sigmoid).then_inc(conv_sig, 1)
                act.wait_ge(conv_step, count(i, CONV_STEPS, 4))
                nc.scalar.copy(o_hi[:, bass.ds(i * 2, 2), :], prod2[:]).then_inc(o_rounded, 1)

            for j in range(1, N_F + 1):
                round_unit(None, 0, U_F + j + LEAD)
            act.wait_ge(f_dve, 1)
            nc.scalar.activation(f_e[:], f_na[:], ACT.Exp).then_inc(f_act, 1)
            act.wait_ge(f_act, 1)
            nc.scalar.activation(f_l[:], f_e[:], ACT.Ln, bias=1.0).then_inc(f_act, 1)
            act.wait_ge(f_dve, 4)
            act.dma_start(neg_c_dram, neg_c[:]).then_inc(c_stored, 16)

            with act.Fori(0, PAIRS) as i:
                for j in range(1, N_MERGE + 1):
                    round_unit(i, N_MERGE, U_MC + j + LEAD)
                    if j == PER:
                        act.wait_ge(w_used, count(i, N_MERGE, RING + U_MC + j))
                        act.wait_ge(free[B], count(i, 1, FREE_B["mc"]))
                        nc.scalar.activation(gate[:], ps[:, A:A + 2, 0:SEQ], ACT.Sigmoid).then_inc(free[A], 1)

            act.wait_ge(c_stored, 16)
            with act.Fori(0, PAIRS) as i:
                for j in range(1, N_ATT + 1):
                    round_unit(i, N_ATT, U_ATT + j + LEAD)
                    if j == 2:
                        act.wait_ge(bias_made, count(i, 1, 1))
                        act.dma_start(neg_cb[:], neg_c_dram[bass.ds(i * 2, 2), :].partition_broadcast(P)
                                      ).then_inc(bias_landed, 16)
                    if j in (PER, 2 * PER, 3 * PER):
                        act.wait_ge(w_used, count(i, N_ATT, RING + U_ATT + j))
                        if j == PER:
                            nc.scalar.copy(k_t[:], ps[:, A:A + 2, 0:TOK]).then_inc(free[A], 1)
                        elif j == 2 * PER:
                            nc.scalar.copy(q_t[:], ps[:, B:B + 2, 0:SEQ]).then_inc(free[B], 1)
                        else:
                            nc.scalar.copy(v_t[:], ps[:, A:A + 2, 0:TOK]).then_inc(free[A], 1)
                    if j == 11:
                        act.wait_ge(att_step, count(i, ATT_STEPS, 2))
                        for b in range(2):
                            for t, keys in enumerate((slice(0, K0), slice(K0, SC))):
                                last = nc.scalar.activation(probs[:, b, keys], probs[:, b, keys], ACT.Exp,
                                                            bias=nmax[:, b, t:t + 1],
                                                            accum_out=den[:, b, t:t + 1])
                        last.then_inc(exp_done, 1)
                    if j == 14:
                        act.wait_ge(v_turned, count(i, 1, 1))
                        nc.scalar.copy(v_nat[:, :, 0:2 * P], ps[:, E:E + 2, 0:2 * P])
                        nc.scalar.copy(v_nat[0:META, :, 2 * P:3 * P], ps[0:META, E:E + 2, 2 * P:3 * P]
                                       ).then_inc(free[E], 1)
                act.wait_ge(w_used, count(i, N_ATT, RING + U_ATT + N_ATT))
                nc.scalar.activation(gate[:], ps[:, B:B + 2, 0:SEQ], ACT.Exp, scale=-1.0).then_inc(z_exp, 1)
                act.wait_ge(free[E], count(i, 2, FREE_E["att"] + 2))
                nc.scalar.copy(o_hi[:, bass.ds(i * 2, 2), :], prod2[:]).then_inc(o_rounded, 1)

            with act.Fori(0, PAIRS) as i:
                for j in range(1, N_MERGE + 1):
                    round_unit(i, N_MERGE, U_MA + j + LEAD)
                    if j == PER:
                        act.wait_ge(w_used, count(i, N_MERGE, RING + U_MA + j))
                        act.wait_ge(free[B], count(i, 1, FREE_B["ma"]))
                        nc.scalar.activation(gate[:], ps[:, A:A + 2, 0:SEQ], ACT.Sigmoid).then_inc(free[A], 1)
                act.wait_ge(merge_step, count(i, 1, 1))
                nc.scalar.copy(m_hi[:, bass.ds(i * 2, 2), :], prod2[:]).then_inc(m_rounded, 1)

            rest = UNITS - (U_OUT + 1 + LEAD)
            with act.Fori(0, rest // RING) as i:
                for j in range(RING):
                    round_unit(i, RING, U_OUT + 1 + LEAD + j)
            for n in range(UNITS - rest % RING, UNITS):
                round_unit(None, 0, n)
            for t in range(2):
                act.wait_ge(y_added, 3 + t)
                nc.scalar.activation(square2[:, t, :], y[:, t, :], ACT.Square, accum_out=sumsq[:, t:t + 1]).then_inc(y_ss, 1)

        @block.vector
        def _(dve):
            def split_unit(i, per, c):
                dve.wait_ge(w_rounded, count(i, per, c + 1))
                nc.vector.tensor_tensor(w_lo[:, c % RING, :], w_raw[:, c % RAW, :],
                                        w_hi[:, c % RING, :].bitcast(F32), ALU.subtract).then_inc(w_split, 1)

            dve.sem_inc(w_split, RAW)
            dve.sem_inc(w_used, RING)
            dve.wait_ge(x_landed[1], 16)
            nc.vector.tensor_tensor_reduce(out=square1[:], in0=x_nat[:, 1, :], in1=x_nat[:, 1, :], scale=1.0,
                                           scalar=0.0, op0=ALU.mult, op1=ALU.add,
                                           accum_out=sumsq[:, 1:2]).then_inc(ss_dve, 1)
            dve.wait_ge(ss_dve, 1)
            dve.wait_ge(ss_act, 1)
            nc.vector.tensor_scalar(var[:, 0:2], sumsq[:, 0:2], 1.0 / D, EPS, ALU.mult, ALU.add).then_inc(var_done, 1)
            dve.wait_ge(ss_act, 2)
            nc.vector.tensor_scalar(var[0:META, 2:3], sumsq[0:META, 2:3], 1.0 / D, EPS, ALU.mult,
                                    ALU.add).then_inc(var_done, 1)
            dve.wait_ge(chan_t, 1)
            nc.vector.tensor_copy(chan[:], ps[:, 7, 0:(TAPS + 1) * KT].rearrange("p (t k) -> p t k", k=KT)
                                  ).then_inc(chan_done, 1)
            dve.wait_ge(rstd_done, 1)
            nc.vector.tensor_scalar(x_nat[:, 1, :], x_nat[:, 1, :], rstd[:, 1:2], None, ALU.mult).then_inc(normed[1], 1)
            dve.wait_ge(rstd_done, 2)
            nc.vector.tensor_scalar(meta_nat[:], meta_nat[:], rstd[0:META, 2:3], None, ALU.mult).then_inc(normed[2], 1)
            split_unit(None, 0, 0)
            split_unit(None, 0, 1)
            dve.wait_ge(chan_done, 1)
            for k in range(KT):
                dve.wait_ge(h_rounded, k + 1)
                nc.vector.scalar_tensor_tensor(out=h_lo[:, k, :], in0=ps[:, k % 8, 0:TOK],
                                               scalar=chan[:, TAPS, k:k + 1], in1=h_hi[:, k, :].bitcast(F32),
                                               op0=ALU.mult, op1=ALU.subtract).then_inc(h_split, 1)
                if k >= 8 and k % 2 == 1:
                    dve.wait_ge(h_split, k + 1)
                    dve.sem_inc(free[k % 8 - 1], 1)
                if k % 4 == 3:
                    split_unit(None, 0, 2 + k // 4)

            with dve.Fori(0, PAIRS) as i:
                def step(n):
                    dve.wait_ge(conv_step, count(i, CONV_STEPS, n))

                for j in range(1, N_CONV + 1):
                    split_unit(i, N_CONV, U_CONV + j + LEAD)
                    if j == 2 * PER:
                        dve.wait_ge(w_used, count(i, N_CONV, RING + U_CONV + j))
                        dve.wait_ge(free[A], count(i, 1, FREE_A["conv"]))
                        nc.vector.tensor_tensor(cu[:], ps[:, B:B + 2, 0:CONV_TOK], u_sb[:], ALU.mult
                                                ).then_inc(free[B], 1)
                        dve.wait_ge(free[B], count(i, 1, FREE_B["conv"] + 1))
                        for tap in range(TAPS):
                            if tap > 0:
                                step(tap)
                            for b in range(2):
                                w = chan[:, tap, bass.ds(i * 2 + b, 1)]
                                shifted = cu[:, b, tap:tap + SEQ]
                                if tap == 0:
                                    last = nc.vector.tensor_scalar(conv[0][:, b, :], shifted, w, None, ALU.mult)
                                else:
                                    last = nc.vector.scalar_tensor_tensor(
                                        out=conv[tap][:, b, :], in0=shifted, scalar=w,
                                        in1=conv[tap - 1][:, b, :], op0=ALU.mult, op1=ALU.add)
                            last.then_inc(conv_step, 1)
                    if j == 3 * PER:
                        dve.wait_ge(w_used, count(i, N_CONV, RING + U_CONV + j))
                        step(3)
                        nc.vector.tensor_tensor(conv_gated[:], ps[:, C:C + 2, 0:SEQ], conv[TAPS - 1][:], ALU.mult
                                                ).then_inc(free[C], 1)
                dve.wait_ge(conv_sig, count(i, 1, 1))
                nc.vector.tensor_tensor(prod[:], ps[:, E:E + 2, 0:SEQ], gate[:], ALU.mult
                                        ).then_inc(free[E], 1)
                dve.wait_ge(free[C], count(i, 1, FREE_C["conv"] + 1))
                dve.wait_ge(free[E], count(i, 1, FREE_E["conv"] + 1))
                nc.vector.tensor_tensor(prod2[:], prod[:], conv_gated[:], ALU.mult).then_inc(conv_step, 1)
                dve.wait_ge(o_rounded, count(i, 1, 1))
                nc.vector.tensor_tensor(o_lo[:, bass.ds(i * 2, 2), :], prod2[:],
                                        o_hi[:, bass.ds(i * 2, 2), :].bitcast(F32), ALU.subtract
                                        ).then_inc(o_split, 1)

            for j in range(1, N_F + 1):
                split_unit(None, 0, U_F + j + LEAD)
            dve.wait_ge(w_used, RING + U_F + N_F)
            dve.wait_ge(bf_landed, 16)
            nc.vector.tensor_scalar(f_x[:], ps[0:HEADS, C, 0:TOK], bf[:], None, ALU.add
                                    ).then_inc(free[C], 1)
            dve.wait_ge(free[C], FREE_C["f"] + 1)
            nc.vector.scalar_tensor_tensor(out=f_na[:], in0=f_x[:], scalar=-1.0, in1=f_x[:], op0=ALU.mult,
                                           op1=ALU.min).then_inc(f_dve, 1)
            nc.vector.memset(f_one[:], 1.0)
            nc.vector.tensor_scalar(f_mn[:], f_x[:], 0.0, None, ALU.min).then_inc(f_dve, 1)
            dve.wait_ge(f_dve, 2)
            dve.wait_ge(f_act, 2)
            nc.vector.tensor_tensor(f_nlog[:], f_l[:], f_mn[:], ALU.subtract).then_inc(f_dve, 1)
            dve.wait_ge(f_dve, 3)
            nc.vector.tensor_tensor_scan(out=neg_c[:], data0=f_one[:], data1=f_nlog[:], initial=0.0,
                                         op0=ALU.mult, op1=ALU.add).then_inc(f_dve, 1)

            with dve.Fori(0, PAIRS) as i:
                for j in range(1, N_MERGE + 1):
                    split_unit(i, N_MERGE, U_MC + j + LEAD)
                dve.wait_ge(w_used, count(i, N_MERGE, RING + U_MC + N_MERGE))
                dve.wait_ge(free[A], count(i, 1, FREE_A["mc"] + 1))
                nc.vector.tensor_tensor(partial[:, bass.ds(i * 2, 2), :], ps[:, B:B + 2, 0:SEQ], gate[:], ALU.mult
                                        ).then_inc(free[B], 1)

            with dve.Fori(0, PAIRS) as i:
                def step(n):
                    dve.wait_ge(att_step, count(i, ATT_STEPS, n))

                for j in range(1, N_ATT + 1):
                    split_unit(i, N_ATT, U_ATT + j + LEAD)
                    if j == 10:
                        dve.wait_ge(s_done, count(i, 1, 1))
                        dve.wait_ge(bias_made, count(i, 1, 2))
                        nc.vector.scalar_tensor_tensor(out=probs[:], in0=ps[:, C:C + 2, 0:SC], scalar=SCALE,
                                                       in1=bias[:], op0=ALU.mult, op1=ALU.add
                                                       ).then_inc(free[C], 1)
                        dve.wait_ge(free[C], count(i, 2, FREE_C["att"] + 1))
                        nc.vector.tensor_reduce(smax[:, :, 0], probs[:, :, 0:K0], AX.X, ALU.max)
                        nc.vector.tensor_reduce(smax[:, :, 1], probs[:, :, K0:SC], AX.X, ALU.max
                                                ).then_inc(att_step, 1)
                        step(1)
                        nc.vector.tensor_scalar(nmax[:], smax[:], -1.0, None, ALU.mult).then_inc(att_step, 1)
                    if j == 12:
                        dve.wait_ge(exp_done, count(i, 1, 1))
                        nc.vector.reciprocal(rden[:], den[:]).then_inc(att_step, 1)
                        step(3)
                        for b in range(2):
                            for t, keys in enumerate((slice(0, K0), slice(K0, SC))):
                                last = nc.vector.tensor_scalar(probs[:, b, keys], probs[:, b, keys],
                                                               rden[:, b, t:t + 1], None, ALU.mult)
                        last.then_inc(att_step, 1)
                    if j == 15:
                        dve.wait_ge(p_turned, count(i, 1, 1))
                        nc.vector.tensor_copy(p_t[:], ps[:, C:C + 2, 0:3 * P])
                        nc.vector.tensor_copy(p_tail[:], ps[0:META, C:C + 2, 3 * P:3 * P + 2 * META]
                                              ).then_inc(free[C], 1)
                dve.wait_ge(z_exp, count(i, 1, 1))
                nc.vector.tensor_scalar(prod[:], gate[:], 1.0, None, ALU.add).then_inc(att_step, 1)
                step(5)
                nc.vector.reciprocal(prod2[:], prod[:]).then_inc(att_step, 1)
                step(6)
                nc.vector.tensor_tensor(prod[:], ps[:, B:B + 2, 0:SEQ], prod2[:], ALU.mult
                                        ).then_inc(free[B], 1)
                dve.wait_ge(free[B], count(i, 2, FREE_B["att"] + 2))
                dve.wait_ge(pv_done, count(i, 1, 1))
                nc.vector.tensor_tensor(prod2[:], ps[:, E:E + 2, 0:SEQ], prod[:], ALU.mult
                                        ).then_inc(free[E], 1)
                dve.wait_ge(o_rounded, count(i, 1, PAIRS + 1))
                nc.vector.tensor_tensor(o_lo[:, bass.ds(i * 2, 2), :], prod2[:],
                                        o_hi[:, bass.ds(i * 2, 2), :].bitcast(F32), ALU.subtract
                                        ).then_inc(o_split, 1)

            with dve.Fori(0, PAIRS) as i:
                for j in range(1, N_MERGE + 1):
                    split_unit(i, N_MERGE, U_MA + j + LEAD)
                dve.wait_ge(w_used, count(i, N_MERGE, RING + U_MA + N_MERGE))
                dve.wait_ge(free[A], count(i, 1, FREE_A["ma"] + 1))
                nc.vector.tensor_tensor(prod[:], ps[:, B:B + 2, 0:SEQ], gate[:], ALU.mult
                                        ).then_inc(free[B], 1)
                dve.wait_ge(free[B], count(i, 1, FREE_B["ma"] + 1))
                nc.vector.tensor_tensor(prod2[:], prod[:], partial[:, bass.ds(i * 2, 2), :], ALU.add
                                        ).then_inc(merge_step, 1)
                dve.wait_ge(m_rounded, count(i, 1, 1))
                nc.vector.tensor_tensor(m_lo[:, bass.ds(i * 2, 2), :], prod2[:],
                                        m_hi[:, bass.ds(i * 2, 2), :].bitcast(F32), ALU.subtract
                                        ).then_inc(m_split, 1)

            rest = UNITS - (U_OUT + 1 + LEAD)
            with dve.Fori(0, rest // RING) as i:
                for j in range(RING):
                    split_unit(i, RING, U_OUT + 1 + LEAD + j)
            for n in range(UNITS - rest % RING, UNITS):
                split_unit(None, 0, n)
            dve.wait_ge(x_res_landed, 16)
            for c in range(2):
                for t in range(2):
                    if t == 0:
                        dve.wait_ge(y_tile, N_OUT - 1 + c)
                    else:
                        dve.wait_ge(w_used, RING + UNITS - 1 + c)
                    bank = OUT_BANK[c] + 2 * t
                    cols = slice(c * UNIT, (c + 1) * UNIT)
                    nc.vector.tensor_tensor(y[:, t, cols], ps[:, bank:bank + 2, :],
                                            x_res[:, t, cols], ALU.add).then_inc(y_added, 1)
            for t in range(2):
                dve.wait_ge(y_ss, t + 1)
                nc.vector.tensor_scalar(var[:, t:t + 1], sumsq[:, t:t + 1], 1.0 / D, EPS, ALU.mult,
                                        ALU.add).then_inc(y_var, 1)
            dve.wait_ge(gain_landed, 16)
            for t in range(2):
                dve.wait_ge(y_rstd, t + 1)
                for c in range(2):
                    cols = slice(c * UNIT, (c + 1) * UNIT)
                    nc.vector.scalar_tensor_tensor(out=y[:, t, cols], in0=y[:, t, cols], scalar=rstd[:, t:t + 1],
                                                   in1=gain_b[:, cols], op0=ALU.mult, op1=ALU.mult
                                                   ).then_inc(y_scaled, 1)

        @block.tensor
        def _(pe):
            def project(i, per, c, bank, rhs_hi, rhs_lo, part, kt0, blocks=2, k_in=UK, last_k=KT):
                pe.wait_ge(w_split, count(i, per, RAW + c + 1))
                width = UNIT // k_in
                cols = part.stop - part.start
                for kk in range(k_in):
                    k = kt0 + kk
                    for b in range(blocks):
                        w = slice(kk * width + b * P, kk * width + (b + 1) * P)
                        dst = ps[:, bank + b, 0:cols]
                        hi, lo = w_hi[:, c % RING, w], w_lo[:, c % RING, w]
                        nc.tensor.matmul(dst, hi, rhs_hi[:, k, part], start=(k == 0), stop=False)
                        nc.tensor.matmul(dst, hi, rhs_lo[:, k, part], start=False, stop=False)
                        last = nc.tensor.matmul(dst, lo, rhs_hi[:, k, part], start=False, stop=(k == KT - 1))
                return last.then_inc(w_used, 1)

            ALL, REAL, CONV = slice(0, TOK), slice(META, TOK), slice(META - TAPS + 1, TOK)

            pe.wait_ge(consts, 1)
            pe.wait_ge(rows_landed, 32)
            rows = (TAPS + 1) * KT
            nc.tensor.transpose(ps[:, 7, 0:rows], chan_rows[:], ident[0:rows, 0:rows]).then_inc(chan_t, 1)
            for k in range(KT):
                if k == 7:
                    pe.wait_ge(chan_done, 1)
                if k >= 8:
                    pe.wait_ge(h_split, k - 7)
                ch = slice(k * P, (k + 1) * P)
                for t in range(2):
                    if k == 0:
                        pe.wait_ge(normed[t], 1)
                    nc.tensor.transpose(ps[:, k % 8, META + t * P:META + (t + 1) * P], x_nat[:, t, ch], ident[:])
                if k == 0:
                    pe.wait_ge(normed[2], 1)
                nc.tensor.transpose(ps[:, k % 8, 0:META], meta_nat[:, ch], ident[0:META, 0:META]
                                    ).then_inc(h_turned, 1)

            pe.wait_ge(h_split, KT)
            with pe.Fori(0, PAIRS) as i:
                for j in range(N_CONV):
                    bank = (A, B, C, E)[j // PER]
                    if j % PER == 0:
                        name = {A: FREE_A, B: FREE_B, C: FREE_C, E: FREE_E}[bank]
                        pe.wait_ge(free[bank], count(i, 1, name["conv"]))
                    part = CONV if j < 2 * PER else REAL
                    project(i, N_CONV, U_CONV + j, bank, h_hi, h_lo, part, j % PER * UK)

            pe.wait_ge(free[C], FREE_C["f"])
            for j in range(N_F):
                project(None, 0, U_F + j, C, h_hi, h_lo, ALL, j * 8, blocks=1, k_in=8)

            pe.wait_ge(o_split, PAIRS)
            with pe.Fori(0, PAIRS) as i:
                for j in range(N_MERGE):
                    bank = (A, B)[j // PER]
                    if j % PER == 0:
                        pe.wait_ge(free[bank], count(i, 1, FREE_A["mc"]))
                    src_hi, src_lo, part = (h_hi, h_lo, REAL) if j < PER else (o_hi, o_lo, slice(0, SEQ))
                    project(i, N_MERGE, U_MC + j, bank, src_hi, src_lo, part, j % PER * UK)

            with pe.Fori(0, PAIRS) as i:
                for j in range(N_ATT):
                    bank = (A, B)[j // PER % 2]
                    if j % PER == 0:
                        pe.wait_ge(free[bank], count(i, 2, FREE_A["att"] + j // (2 * PER)))
                    part = REAL if j // PER in (1, 3) else ALL
                    project(i, N_ATT, U_ATT + j, bank, h_hi, h_lo, part, j % PER * UK)
                    if j == 9:
                        pe.wait_ge(free[B], count(i, 2, FREE_B["att"] + 1))
                        pe.wait_ge(free[C], count(i, 2, FREE_C["att"]))
                        for b in range(2):
                            nc.tensor.matmul(ps[:, C + b, 0:K0], q_t[:, b, 0:P], k_t[:, b, 0:K0],
                                             start=True, stop=True)
                            last = nc.tensor.matmul(ps[:, C + b, K0:SC], q_t[:, b, P:2 * P], k_t[:, b, :],
                                                    start=True, stop=True)
                        last.then_inc(s_done, 1)
                    if j == 12:
                        pe.wait_ge(free[A], count(i, 2, FREE_A["att"] + 2))
                        pe.wait_ge(free[E], count(i, 2, FREE_E["att"]))
                        for b in range(2):
                            for t in range(3):
                                toks = slice(t * P, min((t + 1) * P, TOK))
                                last = nc.tensor.transpose(ps[0:toks.stop - toks.start, E + b, t * P:(t + 1) * P],
                                                           v_t[:, b, toks], ident[:])
                        last.then_inc(v_turned, 1)
                    if j == 13:
                        pe.wait_ge(att_step, count(i, ATT_STEPS, 4))
                        pe.wait_ge(free[C], count(i, 2, FREE_C["att"] + 1))
                        for b in range(2):
                            nc.tensor.transpose(ps[:, C + b, 0:P], probs[:, b, 0:P], ident[:])
                            nc.tensor.transpose(ps[:, C + b, P:2 * P], probs[:, b, K0:K0 + P], ident[:])
                            nc.tensor.transpose(ps[:, C + b, 2 * P:3 * P], probs[:, b, K0 + P:K0 + 2 * P], ident[:])
                            for t, keys in enumerate((slice(P, K0), slice(SC - META, SC))):
                                tail = slice(3 * P + t * META, 3 * P + (t + 1) * META)
                                last = nc.tensor.matmul(ps[0:META, C + b, tail], probs[:, b, keys],
                                                        ident[:, P - META:P], start=True, stop=True)
                        last.then_inc(p_turned, 1)
                pe.wait_ge(free[C], count(i, 2, FREE_C["att"] + 2))
                pe.wait_ge(free[E], count(i, 2, FREE_E["att"] + 1))
                for b in range(2):
                    o = ps[:, E + b, 0:SEQ]
                    nc.tensor.matmul(o, v_nat[:, b, 0:P], p_t[:, b, 0:2 * P], start=True, stop=False)
                    nc.tensor.matmul(o[:, P - META:P], v_nat[0:META, b, P:2 * P], p_tail[:, b, 0:META],
                                     start=False, stop=False)
                    nc.tensor.matmul(o[:, P:2 * P], v_nat[:, b, P:2 * P], p_t[:, b, 2 * P:3 * P],
                                     start=False, stop=False)
                    last = nc.tensor.matmul(o[:, 2 * P - META:2 * P], v_nat[0:META, b, 2 * P:3 * P],
                                            p_tail[:, b, META:2 * META], start=False, stop=True)
                last.then_inc(pv_done, 1)

            with pe.Fori(0, PAIRS) as i:
                for j in range(N_MERGE):
                    bank = (A, B)[j // PER]
                    if j % PER == 0:
                        pe.wait_ge(free[bank], count(i, 1, FREE_A["ma"]))
                    if j == PER:
                        pe.wait_ge(o_split, 2 * PAIRS)
                    src_hi, src_lo, part = (h_hi, h_lo, REAL) if j < PER else (o_hi, o_lo, slice(0, SEQ))
                    project(i, N_MERGE, U_MA + j, bank, src_hi, src_lo, part, j % PER * UK)

            for u in range(N_OUT):
                k, c = u // 2, u % 2
                if u < 2:
                    for bank, name in (((C, FREE_C), (E, FREE_E)), ((A, FREE_A), (B, FREE_B)))[u]:
                        pe.wait_ge(free[bank], name["out"])
                if c == 0 and k % 2 == 0:
                    pe.wait_ge(m_split, k // 2 + 1)
                pe.wait_ge(w_split, RAW + U_OUT + u + 1)
                slot = (U_OUT + u) % RING
                for t in range(2):
                    toks = slice(t * P, (t + 1) * P)
                    for q in range(2):
                        dst = ps[:, OUT_BANK[c] + 2 * t + q, :]
                        w = slice(q * 512, (q + 1) * 512)
                        nc.tensor.matmul(dst, m_hi[:, k, toks], w_hi[:, slot, w], start=(k == 0), stop=False)
                        nc.tensor.matmul(dst, m_hi[:, k, toks], w_lo[:, slot, w], start=False, stop=False)
                        last = nc.tensor.matmul(dst, m_lo[:, k, toks], w_hi[:, slot, w], start=False,
                                                stop=(k == KT - 1))
                    last.then_inc(y_tile if t == 0 else w_used, 1)


_INS = ["x", "meta_tokens", "norm_gain", "w_in", "b_f", "conv_w", "w_att_o", "w_conv_o", "w_out", "final_gain"]


def kernel(**inputs):
    import numpy as np
    import concourse.bacc as bacc
    from concourse.bass_utils import run_bass_kernel_spmd

    nc = bacc.Bacc("TRN2", target_bir_lowering=False, num_devices=1)
    arrays, args = {}, []
    for name in _INS:
        a = np.ascontiguousarray(inputs[name])
        if name in ("x", "w_in", "conv_w", "w_att_o", "w_conv_o", "w_out"):
            a = a.reshape(a.shape[1:])
        arrays[f"in_{name}"] = a
        args.append(nc.dram_tensor(f"in_{name}", a.shape, mybir.dt.from_np(a.dtype), kind="ExternalInput").ap())
    neg_c_dram = nc.dram_tensor("neg_c_dram", (HEADS, TOK), F32, kind="Internal").ap()
    out = nc.dram_tensor("out", (SEQ, D), F32, kind="ExternalOutput").ap()
    hybrid_block(nc, *args, neg_c_dram, out)
    r = run_bass_kernel_spmd(nc, [arrays], core_ids=[0])
    return r.results[0]["out"].reshape(1, SEQ, D)
```

```python
from contextlib import ExitStack

import concourse.bass as bass
from concourse import mybir

F32 = mybir.dt.float32
F32R = mybir.dt.float32r
ALU = mybir.AluOpType
ACT = mybir.ActivationFunctionType
AX = mybir.AxisListType

P = 128
D = 2048
SEQ = 256
META = 16
TOK = META + SEQ
HEADS = 16
DH = 128
TAPS = 3
EPS = 1e-6
SCALE = DH ** -0.5
NEG = -1e30

KT = D // P
PAIRS = KT // 2
CONV_TOK = SEQ + TAPS - 1

COL_Q, COL_K, COL_V, COL_F = 0, D, 2 * D, 3 * D
COL_Z = COL_F + HEADS
COL_U, COL_GB, COL_GC, COL_ZC = COL_Z + D, COL_Z + 2 * D, COL_Z + 3 * D, COL_Z + 4 * D
COL_MA, COL_MC = COL_Z + 5 * D, COL_Z + 6 * D

UNIT = 1024
RAW, RING, LEAD = 4, 8, 5
UK = 4
PER = KT // UK
N_CONV, N_F, N_MERGE, N_ATT, N_OUT = 4 * PER, 2, 2 * PER, 4 * PER, 2 * KT
U_CONV = 0
U_F = U_CONV + N_CONV * PAIRS
U_MC = U_F + N_F
U_ATT = U_MC + N_MERGE * PAIRS
U_MA = U_ATT + N_ATT * PAIRS
U_OUT = U_MA + N_MERGE * PAIRS
UNITS = U_OUT + N_OUT
OUT_STEP = 8
OUT_K = OUT_STEP // 2
HALF = 512

K0 = META + P
SC = K0 + TOK

OUT_BANK = (4, 0)
A, B, C, E = 0, 2, 4, 6
FREE_A = {"conv": 1, "mc": 1 + PAIRS, "att": 1 + 2 * PAIRS, "ma": 1 + 4 * PAIRS, "out": 1 + 5 * PAIRS}
FREE_B = FREE_A
FREE_C = {"conv": 1, "f": 1 + PAIRS, "att": 2 + PAIRS, "out": 2 + 3 * PAIRS}
FREE_E = {"conv": 1, "att": 1 + PAIRS, "out": 1 + 3 * PAIRS}


def hybrid_block(nc, x, meta_tokens, norm_gain, w_in, b_f, conv_w, w_att_o, w_conv_o, w_out,
                 final_gain, neg_c_dram, out):
    at, end = {}, {}
    base = (nc.sbuf_base + 31) // 32 * 32

    def region(name, size):
        nonlocal base
        at[name] = base
        base += size
        end[name] = base

    region("h", 2 * KT * TOK * 4)
    region("o", 2 * KT * SEQ * 4)
    region("p", KT * SEQ * 4)
    region("m", 2 * KT * SEQ * 4)
    region("raw", RAW * UNIT * 4)
    region("hi", RING * UNIT * 4)
    region("lo", RING * UNIT * 4)
    region("misc", 13 * 1024)

    def place(reg, name, shape, dtype=F32):
        t = nc.alloc_sbuf_tensor_at(name, shape, dtype, offset=at[reg])
        size = 4
        for s in shape[1:]:
            size *= s
        at[reg] += (size + 31) // 32 * 32
        assert at[reg] <= end[reg], name
        return t

    misc = lambda name, shape, dtype=F32: place("misc", name, shape, dtype)
    ident = misc("ident", [P, P])
    chan_rows = misc("chan_rows", [(TAPS + 1) * KT, P])
    chan = misc("chan", [P, TAPS + 1, KT])
    bf = misc("bf", [HEADS, 1])
    mask = misc("mask", [P, SC])
    gate = misc("gate", [P, 2, SEQ])
    prod = misc("prod", [P, 2, SEQ])
    prod2 = misc("prod2", [P, 2, SEQ])
    sumsq = misc("sumsq", [P, 2, 2])
    sums = misc("sums", [P, 2])
    warm_up = misc("warm_up", [P, 4])
    meta_sumsq = misc("meta_sumsq", [META, 1])
    y_sumsq = misc("y_sumsq", [P, 8])
    y_mean = misc("y_mean", [P, 8])
    var = misc("var", [P, 4])
    minus_half = misc("minus_half", [P, 4])
    rstd = misc("rstd", [P, 4])
    nmax = misc("nmax", [P, 2, 2])
    smax = misc("smax", [P, 2, 2])
    den = misc("den", [P, 2, 2])
    rden = misc("rden", [P, 2, 2])

    w_raw = place("raw", "w_raw", [P, RAW, UNIT])
    w_hi = place("hi", "w_hi", [P, RING, UNIT], F32R)
    w_lo = place("lo", "w_lo", [P, RING, UNIT], F32R)

    h_at, o_at, m_at = at["h"], at["o"], at["m"]
    x_nat = place("o", "x_nat", [P, 2, D])
    meta_nat = place("o", "meta_nat", [META, D])
    square = place("m", "square", [P, 2, D])
    p_at = at["p"]
    square_meta = place("p", "square_meta", [META, D])
    at["o"], at["m"], at["p"] = o_at, m_at, p_at
    h_hi = place("h", "h_hi", [P, KT, TOK], F32R)
    h_lo = place("h", "h_lo", [P, KT, TOK], F32R)
    o_hi = place("o", "o_hi", [P, KT, SEQ], F32R)
    o_lo = place("o", "o_lo", [P, KT, SEQ], F32R)
    partial = place("p", "partial", [P, KT, SEQ])
    u_sb = place("m", "u_sb", [P, 2, CONV_TOK])
    cu = place("m", "cu", [P, 2, CONV_TOK])
    conv = [place("m", f"conv{j}", [P, 2, SEQ]) for j in range(TAPS)]
    conv_gated = place("m", "conv_gated", [P, 2, SEQ])
    at["m"] = m_at
    f_x = place("m", "f_x", [HEADS, TOK])
    f_na = place("m", "f_na", [HEADS, TOK])
    f_e = place("m", "f_e", [HEADS, TOK])
    f_l = place("m", "f_l", [HEADS, TOK])
    f_mn = place("m", "f_mn", [HEADS, TOK])
    f_nlog = place("m", "f_nlog", [HEADS, TOK])
    f_one = place("m", "f_one", [HEADS, TOK])
    neg_c = place("m", "neg_c", [HEADS, TOK])
    at["m"] = m_at
    neg_cb = place("m", "neg_cb", [P, 2, TOK])
    bias = place("m", "bias", [P, 2, SC])
    k_hi = place("m", "k_hi", [P, 2, TOK], F32R)
    k_lo = place("m", "k_lo", [P, 2, TOK], F32R)
    q_hi = place("m", "q_hi", [P, 2, SEQ], F32R)
    q_lo = place("m", "q_lo", [P, 2, SEQ], F32R)
    v_t = place("m", "v_t", [P, 2, TOK])
    v_hi = place("m", "v_hi", [P, 2, 3 * P], F32R)
    v_lo = place("m", "v_lo", [P, 2, 3 * P], F32R)
    probs = place("m", "probs", [P, 2, SC])
    p_hi = place("m", "p_hi", [P, 2, 3 * P], F32R)
    p_lo = place("m", "p_lo", [P, 2, 3 * P], F32R)
    tail_hi = place("m", "tail_hi", [META, 2, 2 * META], F32R)
    tail_lo = place("m", "tail_lo", [META, 2, 2 * META], F32R)
    at["m"] = m_at
    m_hi = place("m", "m_hi", [P, KT, SEQ], F32R)
    m_lo = place("m", "m_lo", [P, KT, SEQ], F32R)
    at["h"], at["o"], at["p"] = h_at, o_at, p_at
    x_res = place("h", "x_res", [P, 2, D])
    gain_b = place("h", "gain_b", [P, D])
    y = place("o", "y", [P, 2, D])
    square2 = place("o", "square2", [P, 2, D])
    y_gain = place("p", "y_gain", [P, 2, D])
    assert base <= nc.sbuf_usable_end

    with ExitStack() as ctx:
        ps = ctx.enter_context(nc.psum_tensor("ps", [P, 8, 512], F32))
        sem = lambda name: ctx.enter_context(nc.semaphore(name))

        x_landed = [[sem(f"x_landed{t}{c}") for c in range(2)] for t in range(2)]
        meta_landed = sem("meta_landed")
        warm = sem("warm")
        rows_landed = sem("rows_landed")
        bf_landed = sem("bf_landed")
        w_landed = [sem(f"w_landed{s}") for s in range(RAW)]
        w_rounded = sem("w_rounded")
        w_split = sem("w_split")
        w_used = sem("w_used")
        free = {A: sem("free_a"), B: sem("free_b"), C: sem("free_c"), E: sem("free_e")}
        consts = sem("consts")
        ones_made = sem("ones_made")
        ss_act, ss_dve = sem("ss_act"), sem("ss_dve")
        var_done, rstd_done = sem("var_done"), sem("rstd_done")
        normed = [sem(f"normed{t}") for t in range(3)]
        chan_t, chan_done = sem("chan_t"), sem("chan_done")
        h_turned, h_rounded, h_split = sem("h_turned"), sem("h_rounded"), sem("h_split")
        conv_step, conv_sig = sem("conv_step"), sem("conv_sig")
        o_rounded, o_split = sem("o_rounded"), sem("o_split")
        f_dve, f_act, c_stored = sem("f_dve"), sem("f_act"), sem("c_stored")
        bias_landed, bias_made = sem("bias_landed"), sem("bias_made")
        kq_rounded, v_rounded, p_rounded = sem("kq_rounded"), sem("v_rounded"), sem("p_rounded")
        s_done, exp_done, v_turned, p_turned, pv_done = (
            sem("s_done"), sem("exp_done"), sem("v_turned"), sem("p_turned"), sem("pv_done"))
        att_step, z_exp = sem("att_step"), sem("z_exp")
        merge_step, m_rounded, m_split = sem("merge_step"), sem("m_rounded"), sem("m_split")
        y_ready = sem("y_ready")
        x_res_landed, gain_landed = sem("x_res_landed"), sem("gain_landed")
        y_added, y_ss, y_gained, y_var, y_rstd = (
            sem("y_added"), sem("y_ss"), sem("y_gained"), sem("y_var"), sem("y_rstd"))
        y_scaled = [sem("y_scaled_left"), sem("y_scaled_right")]
        stored = sem("stored")

        block = ctx.enter_context(nc.Block())

        CONV_STEPS = 4
        ATT_STEPS = 6

        Y_PIECES = [(0, slice(0, UNIT)), (0, slice(UNIT, D)),
                    (1, slice(0, UNIT)), (1, slice(UNIT, UNIT + HALF)), (1, slice(UNIT + HALF, D))]
        Y_READY = (2, 4, 6, 7, 8)
        Y_LAST = (1, 4)

        def h_bank(k):
            return 2 + k % 6

        def count(i, per, c):
            return c if i is None else i * per + c

        @block.sync
        def _(sp):
            def load(i, per, c, src, k=UK):
                sp.wait_ge(w_split, count(i, per, c + 1))
                dst = w_raw[:, c % RAW, :].rearrange("p (k n) -> p k n", k=k)
                sp.dma_start(dst, src).then_inc(w_landed[c % RAW], 16)

            def load_stage(first, sources):
                per = PER * len(sources)
                with sp.Fori(1, PAIRS + 1) as i:
                    for j in range(per):
                        w_k, col = sources[j // PER]
                        rows = slice(j % PER * UK, j % PER * UK + UK)
                        load(i, per, first + j - per,
                             w_k[:, rows, bass.ds(i * (2 * P) + (col - 2 * P), 2 * P)])

            w_in_k, w_conv_k, w_att_k, w_out_k = (
                w.rearrange("(k p) n -> p k n", p=P) for w in (w_in, w_conv_o, w_att_o, w_out))
            for t in range(2):
                for c in range(2):
                    cols = slice(c * D // 2, (c + 1) * D // 2)
                    sp.dma_start(x_nat[:, t, cols], x[t * P:(t + 1) * P, cols]).then_inc(x_landed[t][c], 16)
            sp.dma_start(chan_rows[0:TAPS * KT, :], conv_w.rearrange("t (k p) -> (t k) p", p=P)
                         ).then_inc(rows_landed, 16)
            sp.dma_start(chan_rows[TAPS * KT:(TAPS + 1) * KT, :], norm_gain.rearrange("a (k p) -> (a k) p", p=P)
                         ).then_inc(rows_landed, 16)
            sp.dma_start(bf[:], b_f.rearrange("a h -> h a")).then_inc(bf_landed, 16)
            load_stage(U_CONV, [(w_in_k, COL_U), (w_in_k, COL_GC), (w_in_k, COL_GB), (w_in_k, COL_ZC)])
            for j in range(N_F):
                load(None, 0, U_F + j, w_in_k[:, j * 8:j * 8 + 8, COL_F:COL_F + P], k=8)
            load_stage(U_MC, [(w_in_k, COL_MC), (w_conv_k, 0)])
            load_stage(U_ATT, [(w_in_k, COL_K), (w_in_k, COL_Q), (w_in_k, COL_V), (w_in_k, COL_Z)])
            load_stage(U_MA, [(w_in_k, COL_MA), (w_att_k, 0)])
            with sp.Fori(0, N_OUT // OUT_STEP) as i:
                for j in range(OUT_STEP):
                    half = slice(j // OUT_K * UNIT, (j // OUT_K + 1) * UNIT)
                    load(i, OUT_STEP, U_OUT + j, w_out_k[:, bass.ds(i * OUT_K + j % OUT_K, 1), half], k=1)
            sp.wait_ge(w_used, RING + U_OUT)
            sp.dma_start(x_res[:], x.rearrange("(t p) d -> p t d", p=P)).then_inc(x_res_landed, 16)
            sp.dma_start(gain_b[:], final_gain.partition_broadcast(P)).then_inc(gain_landed, 16)
            for t in range(2):
                for side, n, cols in ((0, 2 * t + 1, slice(0, HALF)), (1, t + 1, slice(UNIT, D)),
                                      (0, 2 * t + 2, slice(HALF, UNIT))):
                    sp.wait_ge(y_scaled[side], n)
                    sp.dma_start(out[t * P:(t + 1) * P, cols], y[:, t, cols]).then_inc(stored, 16)
            sp.wait_ge(stored, 6 * 16)

        @block.gpsimd
        def _(pool):
            nc.gpsimd.memset(ident[:], 1.0).then_inc(ones_made, 1)
            nc.gpsimd.memset(mask[:], 0.0).then_inc(ones_made, 1)
            nc.gpsimd.memset(minus_half[:], -0.5).then_inc(ones_made, 1)
            pool.wait_ge(ones_made, 3)
            nc.gpsimd.affine_select(out=ident[:], in_=ident[:], pattern=[[-1, P]], compare_op=ALU.is_equal,
                                    fill=0.0, base=0, channel_multiplier=1).then_inc(consts, 1)
            nc.gpsimd.affine_select(out=mask[:, 0:K0], in_=mask[:, 0:K0], pattern=[[-1, K0]],
                                    compare_op=ALU.is_ge, fill=NEG, base=META, channel_multiplier=1)
            nc.gpsimd.affine_select(out=mask[:, K0:SC], in_=mask[:, K0:SC], pattern=[[-1, TOK]],
                                    compare_op=ALU.is_ge, fill=NEG, base=K0, channel_multiplier=1
                                    ).then_inc(consts, 1)
            for n, (t, rows) in enumerate(((2, META), (0, P), (1, P))):
                pool.wait_ge(var_done, n + 1)
                nc.gpsimd.tensor_tensor(rstd[0:rows, t:t + 1], var[0:rows, t:t + 1], minus_half[0:rows, t:t + 1],
                                        ALU.pow).then_inc(rstd_done, 1)
            pool.wait_ge(consts, 2)
            pool.sem_inc(bias_made, 1)
            with pool.Fori(0, PAIRS) as i:
                pool.wait_ge(bias_landed, i * 16 + 16)
                pool.wait_ge(free[C], i * 2 + FREE_C["att"])
                for b in range(2):
                    nc.gpsimd.tensor_tensor(bias[:, b, 0:K0], mask[:, 0:K0], neg_cb[:, b, 0:K0], ALU.add)
                    last = nc.gpsimd.tensor_tensor(bias[:, b, K0:SC], mask[:, K0:SC], neg_cb[:, b, :], ALU.add)
                last.then_inc(bias_made, 1)
            for t, n in enumerate(Y_LAST):
                pool.wait_ge(y_var, n + 1)
                nc.gpsimd.tensor_tensor(rstd[:, t:t + 1], y_mean[:, n:n + 1], minus_half[:, t:t + 1],
                                        ALU.pow).then_inc(y_rstd, 1)

        @block.scalar
        def _(act):
            def round_unit(i, per, c):
                act.wait_ge(w_landed[c % RAW], count(i, per // RAW * 16, c // RAW * 16 + 16))
                act.wait_ge(w_used, count(i, per, c + 1))
                nc.scalar.copy(w_hi[:, c % RING, :], w_raw[:, c % RAW, :]).then_inc(w_rounded, 1)

            act.dma_start(meta_nat[:], meta_tokens).then_inc(meta_landed, 16)
            act.wait_ge(ones_made, 3)
            nc.scalar.activation(warm_up[:], minus_half[:], ACT.Square).then_inc(warm, 1)
            for t in range(2):
                for c in range(2):
                    cols = slice(c * D // 2, (c + 1) * D // 2)
                    act.wait_ge(x_landed[t][c], 16)
                    nc.scalar.activation(square[:, t, cols], x_nat[:, t, cols], ACT.Square,
                                         accum_out=sumsq[:, t, c:c + 1]).then_inc(ss_act, 1)
            round_unit(None, 0, 0)
            act.wait_ge(chan_done, 1)
            for k in range(KT):
                act.wait_ge(h_turned, k + 1)
                nc.scalar.activation(h_hi[:, k, :], ps[:, h_bank(k), 0:TOK], ACT.Copy,
                                     scale=chan[:, TAPS, k:k + 1]).then_inc(h_rounded, 1)
                if k % UK == UK - 1:
                    round_unit(None, 0, k // UK + 1)
            for n in range(PER + 1, LEAD + 1):
                round_unit(None, 0, n)

            with act.Fori(0, PAIRS) as i:
                for j in range(1, N_CONV + 1):
                    round_unit(i, N_CONV, U_CONV + j + LEAD)
                    if j == PER:
                        act.wait_ge(w_used, count(i, N_CONV, RING + U_CONV + j))
                        nc.scalar.copy(u_sb[:], ps[:, A:A + 2, 0:CONV_TOK]).then_inc(free[A], 1)
                act.wait_ge(w_used, count(i, N_CONV, RING + U_CONV + N_CONV))
                nc.scalar.activation(gate[:], ps[:, E:E + 2, 0:SEQ], ACT.Sigmoid).then_inc(conv_sig, 1)
                act.wait_ge(conv_step, count(i, CONV_STEPS, 4))
                nc.scalar.copy(o_hi[:, bass.ds(i * 2, 2), :], prod2[:]).then_inc(o_rounded, 1)

            for j in range(1, N_F + 1):
                round_unit(None, 0, U_F + j + LEAD)
            act.wait_ge(f_dve, 1)
            nc.scalar.activation(f_e[:], f_na[:], ACT.Exp).then_inc(f_act, 1)
            act.wait_ge(f_act, 1)
            nc.scalar.activation(f_l[:], f_e[:], ACT.Ln, bias=1.0).then_inc(f_act, 1)
            act.wait_ge(f_dve, 4)
            act.dma_start(neg_c_dram, neg_c[:]).then_inc(c_stored, 16)

            with act.Fori(0, PAIRS) as i:
                for j in range(1, N_MERGE + 1):
                    round_unit(i, N_MERGE, U_MC + j + LEAD)
                    if j == PER:
                        act.wait_ge(w_used, count(i, N_MERGE, RING + U_MC + j))
                        act.wait_ge(free[B], count(i, 1, FREE_B["mc"]))
                        nc.scalar.activation(gate[:], ps[:, A:A + 2, 0:SEQ], ACT.Sigmoid).then_inc(free[A], 1)

            act.wait_ge(c_stored, 16)
            with act.Fori(0, PAIRS) as i:
                for j in range(1, N_ATT + 1):
                    round_unit(i, N_ATT, U_ATT + j + LEAD)
                    if j == 2:
                        act.wait_ge(bias_made, count(i, 1, 1))
                        act.dma_start(neg_cb[:], neg_c_dram[bass.ds(i * 2, 2), :].partition_broadcast(P)
                                      ).then_inc(bias_landed, 16)
                    if j in (PER, 2 * PER, 3 * PER):
                        act.wait_ge(w_used, count(i, N_ATT, RING + U_ATT + j))
                        if j == PER:
                            nc.scalar.copy(k_hi[:], ps[:, A:A + 2, 0:TOK]).then_inc(kq_rounded, 1)
                        elif j == 2 * PER:
                            nc.scalar.copy(q_hi[:], ps[:, B:B + 2, 0:SEQ]).then_inc(kq_rounded, 1)
                        else:
                            nc.scalar.copy(v_t[:], ps[:, A:A + 2, 0:TOK]).then_inc(free[A], 1)
                    if j == 11:
                        act.wait_ge(att_step, count(i, ATT_STEPS, 2))
                        for b in range(2):
                            for t, keys in enumerate((slice(0, K0), slice(K0, SC))):
                                last = nc.scalar.activation(probs[:, b, keys], probs[:, b, keys], ACT.Exp,
                                                            bias=nmax[:, b, t:t + 1],
                                                            accum_out=den[:, b, t:t + 1])
                        last.then_inc(exp_done, 1)
                    if j == 14:
                        act.wait_ge(v_turned, count(i, 1, 1))
                        nc.scalar.copy(v_hi[:, :, 0:2 * P], ps[:, E:E + 2, 0:2 * P])
                        nc.scalar.copy(v_hi[0:META, :, 2 * P:3 * P], ps[0:META, E:E + 2, 2 * P:3 * P]
                                       ).then_inc(v_rounded, 1)
                    if j == 15:
                        act.wait_ge(p_turned, count(i, 1, 1))
                        nc.scalar.copy(p_hi[:], ps[:, C:C + 2, 0:3 * P])
                        nc.scalar.copy(tail_hi[:], ps[0:META, C:C + 2, 3 * P:3 * P + 2 * META]
                                       ).then_inc(p_rounded, 1)
                act.wait_ge(w_used, count(i, N_ATT, RING + U_ATT + N_ATT))
                nc.scalar.activation(gate[:], ps[:, B:B + 2, 0:SEQ], ACT.Exp, scale=-1.0).then_inc(z_exp, 1)
                act.wait_ge(free[E], count(i, 2, FREE_E["att"] + 2))
                nc.scalar.copy(o_hi[:, bass.ds(i * 2, 2), :], prod2[:]).then_inc(o_rounded, 1)

            with act.Fori(0, PAIRS) as i:
                for j in range(1, N_MERGE + 1):
                    round_unit(i, N_MERGE, U_MA + j + LEAD)
                    if j == PER:
                        act.wait_ge(w_used, count(i, N_MERGE, RING + U_MA + j))
                        act.wait_ge(free[B], count(i, 1, FREE_B["ma"]))
                        nc.scalar.activation(gate[:], ps[:, A:A + 2, 0:SEQ], ACT.Sigmoid).then_inc(free[A], 1)
                act.wait_ge(merge_step, count(i, 1, 1))
                nc.scalar.copy(m_hi[:, bass.ds(i * 2, 2), :], prod2[:]).then_inc(m_rounded, 1)

            rest = UNITS - (U_OUT + 1 + LEAD)
            with act.Fori(0, rest // RING) as i:
                for j in range(RING):
                    round_unit(i, RING, U_OUT + 1 + LEAD + j)
            for n in range(UNITS - rest % RING, UNITS):
                round_unit(None, 0, n)
            for n, (t, cols) in enumerate(Y_PIECES):
                act.wait_ge(y_added, n + 1)
                nc.scalar.activation(square2[:, t, cols], y[:, t, cols], ACT.Square,
                                     accum_out=y_sumsq[:, n:n + 1]).then_inc(y_ss, 1)
                if n in Y_LAST:
                    act.wait_ge(y_rstd, t + 1)
                    for cols in (slice(0, HALF), slice(HALF, UNIT)):
                        nc.scalar.activation(y[:, t, cols], y_gain[:, t, cols], ACT.Copy, scale=rstd[:, t:t + 1]
                                             ).then_inc(y_scaled[0], 1)

        @block.vector
        def _(dve):
            def split_unit(i, per, c):
                dve.wait_ge(w_rounded, count(i, per, c + 1))
                nc.vector.tensor_tensor(w_lo[:, c % RING, :], w_raw[:, c % RAW, :],
                                        w_hi[:, c % RING, :].bitcast(F32), ALU.subtract).then_inc(w_split, 1)

            dve.sem_inc(w_split, RAW)
            dve.sem_inc(w_used, RING)
            dve.wait_ge(meta_landed, 16)
            nc.vector.tensor_tensor_reduce(out=square_meta[:], in0=meta_nat[:], in1=meta_nat[:], scale=1.0,
                                           scalar=0.0, op0=ALU.mult, op1=ALU.add,
                                           accum_out=meta_sumsq[:]).then_inc(ss_dve, 1)
            dve.wait_ge(ss_dve, 1)
            nc.vector.tensor_scalar(var[0:META, 2:3], meta_sumsq[:], 1.0 / D, EPS, ALU.mult,
                                    ALU.add).then_inc(var_done, 1)
            dve.wait_ge(rstd_done, 1)
            nc.vector.tensor_scalar(meta_nat[:], meta_nat[:], rstd[0:META, 2:3], None, ALU.mult
                                    ).then_inc(normed[2], 1)
            for t in range(2):
                dve.wait_ge(ss_act, 2 * t + 2)
                nc.vector.tensor_tensor(sums[:, t:t + 1], sumsq[:, t, 0:1], sumsq[:, t, 1:2], ALU.add
                                        ).then_inc(ss_dve, 1)
                dve.wait_ge(ss_dve, t + 2)
                nc.vector.tensor_scalar(var[:, t:t + 1], sums[:, t:t + 1], 1.0 / D, EPS, ALU.mult,
                                        ALU.add).then_inc(var_done, 1)
                dve.wait_ge(rstd_done, t + 2)
                for c in range(4):
                    cols = slice(c * D // 4, (c + 1) * D // 4)
                    nc.vector.tensor_scalar(x_nat[:, t, cols], x_nat[:, t, cols], rstd[:, t:t + 1], None, ALU.mult
                                            ).then_inc(normed[t], 1)
                if t == 0:
                    dve.wait_ge(chan_t, 1)
                    nc.vector.tensor_copy(chan[:], ps[:, 0, 0:(TAPS + 1) * KT].rearrange("p (t k) -> p t k", k=KT)
                                          ).then_inc(chan_done, 1)
            dve.wait_ge(chan_done, 1)
            for k in range(KT):
                if k % 4 == 0:
                    split_unit(None, 0, k // 4)
                dve.wait_ge(h_rounded, k + 1)
                nc.vector.scalar_tensor_tensor(out=h_lo[:, k, :], in0=ps[:, h_bank(k), 0:TOK],
                                               scalar=chan[:, TAPS, k:k + 1], in1=h_hi[:, k, :].bitcast(F32),
                                               op0=ALU.mult, op1=ALU.subtract).then_inc(h_split, 1)
            dve.wait_ge(h_split, KT)
            for bank in (A, B, C, E):
                dve.sem_inc(free[bank], 1)
            for n in range(KT // UK, LEAD + 1):
                split_unit(None, 0, n)

            with dve.Fori(0, PAIRS) as i:
                def step(n):
                    dve.wait_ge(conv_step, count(i, CONV_STEPS, n))

                for j in range(1, N_CONV + 1):
                    split_unit(i, N_CONV, U_CONV + j + LEAD)
                    if j == 2 * PER:
                        dve.wait_ge(w_used, count(i, N_CONV, RING + U_CONV + j))
                        dve.wait_ge(free[A], count(i, 1, FREE_A["conv"]))
                        nc.vector.tensor_tensor(cu[:], ps[:, B:B + 2, 0:CONV_TOK], u_sb[:], ALU.mult
                                                ).then_inc(free[B], 1)
                        dve.wait_ge(free[B], count(i, 1, FREE_B["conv"] + 1))
                        for tap in range(TAPS):
                            if tap > 0:
                                step(tap)
                            for b in range(2):
                                w = chan[:, tap, bass.ds(i * 2 + b, 1)]
                                shifted = cu[:, b, tap:tap + SEQ]
                                if tap == 0:
                                    last = nc.vector.tensor_scalar(conv[0][:, b, :], shifted, w, None, ALU.mult)
                                else:
                                    last = nc.vector.scalar_tensor_tensor(
                                        out=conv[tap][:, b, :], in0=shifted, scalar=w,
                                        in1=conv[tap - 1][:, b, :], op0=ALU.mult, op1=ALU.add)
                            last.then_inc(conv_step, 1)
                    if j == 3 * PER:
                        dve.wait_ge(w_used, count(i, N_CONV, RING + U_CONV + j))
                        step(3)
                        nc.vector.tensor_tensor(conv_gated[:], ps[:, C:C + 2, 0:SEQ], conv[TAPS - 1][:], ALU.mult
                                                ).then_inc(free[C], 1)
                dve.wait_ge(conv_sig, count(i, 1, 1))
                nc.vector.tensor_tensor(prod[:], ps[:, E:E + 2, 0:SEQ], gate[:], ALU.mult
                                        ).then_inc(free[E], 1)
                dve.wait_ge(free[C], count(i, 1, FREE_C["conv"] + 1))
                dve.wait_ge(free[E], count(i, 1, FREE_E["conv"] + 1))
                nc.vector.tensor_tensor(prod2[:], prod[:], conv_gated[:], ALU.mult).then_inc(conv_step, 1)
                dve.wait_ge(o_rounded, count(i, 1, 1))
                nc.vector.tensor_tensor(o_lo[:, bass.ds(i * 2, 2), :], prod2[:],
                                        o_hi[:, bass.ds(i * 2, 2), :].bitcast(F32), ALU.subtract
                                        ).then_inc(o_split, 1)

            for j in range(1, N_F + 1):
                split_unit(None, 0, U_F + j + LEAD)
            dve.wait_ge(w_used, RING + U_F + N_F)
            dve.wait_ge(bf_landed, 16)
            nc.vector.tensor_scalar(f_x[:], ps[0:HEADS, C, 0:TOK], bf[:], None, ALU.add
                                    ).then_inc(free[C], 1)
            dve.wait_ge(free[C], FREE_C["f"] + 1)
            nc.vector.scalar_tensor_tensor(out=f_na[:], in0=f_x[:], scalar=-1.0, in1=f_x[:], op0=ALU.mult,
                                           op1=ALU.min).then_inc(f_dve, 1)
            nc.vector.memset(f_one[:], 1.0)
            nc.vector.tensor_scalar(f_mn[:], f_x[:], 0.0, None, ALU.min).then_inc(f_dve, 1)
            dve.wait_ge(f_dve, 2)
            dve.wait_ge(f_act, 2)
            nc.vector.tensor_tensor(f_nlog[:], f_l[:], f_mn[:], ALU.subtract).then_inc(f_dve, 1)
            dve.wait_ge(f_dve, 3)
            nc.vector.tensor_tensor_scan(out=neg_c[:], data0=f_one[:], data1=f_nlog[:], initial=0.0,
                                         op0=ALU.mult, op1=ALU.add).then_inc(f_dve, 1)

            with dve.Fori(0, PAIRS) as i:
                for j in range(1, N_MERGE + 1):
                    split_unit(i, N_MERGE, U_MC + j + LEAD)
                dve.wait_ge(w_used, count(i, N_MERGE, RING + U_MC + N_MERGE))
                dve.wait_ge(free[A], count(i, 1, FREE_A["mc"] + 1))
                nc.vector.tensor_tensor(partial[:, bass.ds(i * 2, 2), :], ps[:, B:B + 2, 0:SEQ], gate[:], ALU.mult
                                        ).then_inc(free[B], 1)

            with dve.Fori(0, PAIRS) as i:
                def step(n):
                    dve.wait_ge(att_step, count(i, ATT_STEPS, n))

                for j in range(1, N_ATT + 1):
                    split_unit(i, N_ATT, U_ATT + j + LEAD)
                    if j == PER:
                        dve.wait_ge(kq_rounded, count(i, 2, 1))
                        nc.vector.tensor_tensor(k_lo[:], ps[:, A:A + 2, 0:TOK], k_hi[:].bitcast(F32), ALU.subtract
                                                ).then_inc(free[A], 1)
                    if j == 2 * PER:
                        dve.wait_ge(kq_rounded, count(i, 2, 2))
                        nc.vector.tensor_tensor(q_lo[:], ps[:, B:B + 2, 0:SEQ], q_hi[:].bitcast(F32), ALU.subtract
                                                ).then_inc(free[B], 1)
                    if j == 14:
                        dve.wait_ge(v_rounded, count(i, 1, 1))
                        nc.vector.tensor_tensor(v_lo[:, :, 0:2 * P], ps[:, E:E + 2, 0:2 * P],
                                                v_hi[:, :, 0:2 * P].bitcast(F32), ALU.subtract)
                        rest = slice(2 * P, 3 * P)
                        nc.vector.tensor_tensor(v_lo[0:META, :, rest], ps[0:META, E:E + 2, rest],
                                                v_hi[0:META, :, rest].bitcast(F32), ALU.subtract
                                                ).then_inc(free[E], 1)
                    if j == 10:
                        dve.wait_ge(s_done, count(i, 1, 1))
                        dve.wait_ge(bias_made, count(i, 1, 2))
                        nc.vector.scalar_tensor_tensor(out=probs[:], in0=ps[:, C:C + 2, 0:SC], scalar=SCALE,
                                                       in1=bias[:], op0=ALU.mult, op1=ALU.add
                                                       ).then_inc(free[C], 1)
                        dve.wait_ge(free[C], count(i, 2, FREE_C["att"] + 1))
                        nc.vector.tensor_reduce(smax[:, :, 0], probs[:, :, 0:K0], AX.X, ALU.max)
                        nc.vector.tensor_reduce(smax[:, :, 1], probs[:, :, K0:SC], AX.X, ALU.max
                                                ).then_inc(att_step, 1)
                        step(1)
                        nc.vector.tensor_scalar(nmax[:], smax[:], -1.0, None, ALU.mult).then_inc(att_step, 1)
                    if j == 12:
                        dve.wait_ge(exp_done, count(i, 1, 1))
                        nc.vector.reciprocal(rden[:], den[:]).then_inc(att_step, 1)
                        step(3)
                        for b in range(2):
                            for t, keys in enumerate((slice(0, K0), slice(K0, SC))):
                                last = nc.vector.tensor_scalar(probs[:, b, keys], probs[:, b, keys],
                                                               rden[:, b, t:t + 1], None, ALU.mult)
                        last.then_inc(att_step, 1)
                    if j == 15:
                        dve.wait_ge(p_rounded, count(i, 1, 1))
                        nc.vector.tensor_tensor(p_lo[:], ps[:, C:C + 2, 0:3 * P], p_hi[:].bitcast(F32),
                                                ALU.subtract)
                        nc.vector.tensor_tensor(tail_lo[:], ps[0:META, C:C + 2, 3 * P:3 * P + 2 * META],
                                                tail_hi[:].bitcast(F32), ALU.subtract).then_inc(free[C], 1)
                dve.wait_ge(z_exp, count(i, 1, 1))
                nc.vector.tensor_scalar(prod[:], gate[:], 1.0, None, ALU.add).then_inc(att_step, 1)
                step(5)
                nc.vector.reciprocal(prod2[:], prod[:]).then_inc(att_step, 1)
                step(6)
                nc.vector.tensor_tensor(prod[:], ps[:, B:B + 2, 0:SEQ], prod2[:], ALU.mult
                                        ).then_inc(free[B], 1)
                dve.wait_ge(free[B], count(i, 2, FREE_B["att"] + 2))
                dve.wait_ge(pv_done, count(i, 1, 1))
                nc.vector.tensor_tensor(prod2[:], ps[:, E:E + 2, 0:SEQ], prod[:], ALU.mult
                                        ).then_inc(free[E], 1)
                dve.wait_ge(o_rounded, count(i, 1, PAIRS + 1))
                nc.vector.tensor_tensor(o_lo[:, bass.ds(i * 2, 2), :], prod2[:],
                                        o_hi[:, bass.ds(i * 2, 2), :].bitcast(F32), ALU.subtract
                                        ).then_inc(o_split, 1)

            with dve.Fori(0, PAIRS) as i:
                for j in range(1, N_MERGE + 1):
                    split_unit(i, N_MERGE, U_MA + j + LEAD)
                dve.wait_ge(w_used, count(i, N_MERGE, RING + U_MA + N_MERGE))
                dve.wait_ge(free[A], count(i, 1, FREE_A["ma"] + 1))
                nc.vector.tensor_tensor(prod[:], ps[:, B:B + 2, 0:SEQ], gate[:], ALU.mult
                                        ).then_inc(free[B], 1)
                dve.wait_ge(free[B], count(i, 1, FREE_B["ma"] + 1))
                nc.vector.tensor_tensor(prod2[:], prod[:], partial[:, bass.ds(i * 2, 2), :], ALU.add
                                        ).then_inc(merge_step, 1)
                dve.wait_ge(m_rounded, count(i, 1, 1))
                nc.vector.tensor_tensor(m_lo[:, bass.ds(i * 2, 2), :], prod2[:],
                                        m_hi[:, bass.ds(i * 2, 2), :].bitcast(F32), ALU.subtract
                                        ).then_inc(m_split, 1)

            rest = UNITS - (U_OUT + 1 + LEAD)
            with dve.Fori(0, rest // RING) as i:
                for j in range(RING):
                    split_unit(i, RING, U_OUT + 1 + LEAD + j)
            for n in range(UNITS - rest % RING, UNITS):
                split_unit(None, 0, n)
            dve.wait_ge(x_res_landed, 16)
            dve.wait_ge(gain_landed, 16)

            for n, (t, cols) in enumerate(Y_PIECES):
                dve.wait_ge(y_ready, Y_READY[n])
                bank = OUT_BANK[cols.start // UNIT] + 2 * t + cols.start % UNIT // HALF
                banks = (cols.stop - cols.start) // HALF
                nc.vector.tensor_tensor(y[:, t, cols], ps[:, bank:bank + banks, :], x_res[:, t, cols], ALU.add
                                        ).then_inc(y_added, 1)
                dve.wait_ge(y_added, n + 1)
                nc.vector.tensor_tensor(y_gain[:, t, cols], y[:, t, cols], gain_b[:, cols], ALU.mult
                                        ).then_inc(y_gained, 1)
                dve.wait_ge(y_ss, n + 1)
                if n == 0 or n - 1 in Y_LAST:
                    last = nc.vector.tensor_scalar(y_mean[:, n:n + 1], y_sumsq[:, n:n + 1], 1.0 / D, EPS,
                                                   ALU.mult, ALU.add)
                else:
                    dve.wait_ge(y_var, n)
                    last = nc.vector.scalar_tensor_tensor(out=y_mean[:, n:n + 1], in0=y_sumsq[:, n:n + 1],
                                                          scalar=1.0 / D, in1=y_mean[:, n - 1:n],
                                                          op0=ALU.mult, op1=ALU.add)
                last.then_inc(y_var, 1)
                if n in Y_LAST:
                    dve.wait_ge(y_gained, n + 1)
                    dve.wait_ge(y_rstd, t + 1)
                    nc.vector.tensor_scalar(y[:, t, UNIT:D], y_gain[:, t, UNIT:D], rstd[:, t:t + 1], None, ALU.mult
                                            ).then_inc(y_scaled[1], 1)

        @block.tensor
        def _(pe):
            def project(i, per, c, bank, rhs_hi, rhs_lo, part, kt0, blocks=2, k_in=UK,
                        before=None, after=None):
                pe.wait_ge(w_split, count(i, per, RAW + c + 1))
                width = UNIT // k_in
                cols = part.stop - part.start
                for kk in range(k_in):
                    k = kt0 + kk
                    if before:
                        before(k)
                    for b in range(blocks):
                        w = slice(kk * width + b * P, kk * width + (b + 1) * P)
                        dst = ps[:, bank + b, 0:cols]
                        hi, lo = w_hi[:, c % RING, w], w_lo[:, c % RING, w]
                        last = product(dst, hi, lo, rhs_hi[:, k, part], rhs_lo[:, k, part],
                                       start=(k == 0), stop=(k == KT - 1))
                        if kk == k_in - 1 and b == blocks - 1:
                            last.then_inc(w_used, 1)
                    if after:
                        after(k)

            def product(dst, a_hi, a_lo, b_hi, b_lo, start=True, stop=True):
                nc.tensor.matmul(dst, a_hi, b_hi, start=start, stop=False)
                nc.tensor.matmul(dst, a_hi, b_lo, start=False, stop=False)
                return nc.tensor.matmul(dst, a_lo, b_hi, start=False, stop=stop)

            ALL, REAL, CONV = slice(0, TOK), slice(META, TOK), slice(META - TAPS + 1, TOK)

            pe.wait_ge(consts, 1)
            pe.wait_ge(rows_landed, 32)
            rows = (TAPS + 1) * KT
            nc.tensor.transpose(ps[:, 0, 0:rows], chan_rows[:], ident[0:rows, 0:rows]).then_inc(chan_t, 1)
            pe.wait_ge(chan_done, 1)

            def turn(k):
                if k >= 6:
                    pe.wait_ge(h_split, k - 5)
                ch = slice(k * P, (k + 1) * P)
                if k == 0:
                    pe.wait_ge(normed[2], 1)
                nc.tensor.transpose(ps[:, h_bank(k), 0:META], meta_nat[:, ch], ident[0:META, 0:META])
                for t in range(2):
                    if k % 4 == 0:
                        pe.wait_ge(normed[t], k // 4 + 1)
                    last = nc.tensor.transpose(ps[:, h_bank(k), META + t * P:META + (t + 1) * P],
                                               x_nat[:, t, ch], ident[:])
                last.then_inc(h_turned, 1)

            def conv_pair(i, first):
                for j in range(first, N_CONV):
                    bank = (A, B, C, E)[j // PER]
                    if j % PER == 0:
                        name = {A: FREE_A, B: FREE_B, C: FREE_C, E: FREE_E}[bank]
                        pe.wait_ge(free[bank], count(i, 1, name["conv"]))
                    part = CONV if j < 2 * PER else REAL
                    project(i, N_CONV, U_CONV + j, bank, h_hi, h_lo, part, j % PER * UK)

            for k in range(6):
                turn(k)
            for j in range(PER):
                def before(k):
                    pe.wait_ge(h_split, k + 1)

                def after(k):
                    if k + 6 < KT:
                        turn(k + 6)

                project(None, 0, U_CONV + j, A, h_hi, h_lo, CONV, j * UK, before=before, after=after)
            conv_pair(None, PER)
            with pe.Fori(1, PAIRS) as i:
                conv_pair(i, 0)

            pe.wait_ge(free[C], FREE_C["f"])
            for j in range(N_F):
                project(None, 0, U_F + j, C, h_hi, h_lo, ALL, j * 8, blocks=1, k_in=8)

            pe.wait_ge(o_split, PAIRS)
            with pe.Fori(0, PAIRS) as i:
                for j in range(N_MERGE):
                    bank = (A, B)[j // PER]
                    if j % PER == 0:
                        pe.wait_ge(free[bank], count(i, 1, FREE_A["mc"]))
                    src_hi, src_lo, part = (h_hi, h_lo, REAL) if j < PER else (o_hi, o_lo, slice(0, SEQ))
                    project(i, N_MERGE, U_MC + j, bank, src_hi, src_lo, part, j % PER * UK)

            with pe.Fori(0, PAIRS) as i:
                for j in range(N_ATT):
                    bank = (A, B)[j // PER % 2]
                    if j % PER == 0:
                        pe.wait_ge(free[bank], count(i, 2, FREE_A["att"] + j // (2 * PER)))
                    part = REAL if j // PER in (1, 3) else ALL
                    project(i, N_ATT, U_ATT + j, bank, h_hi, h_lo, part, j % PER * UK)
                    if j == 9:
                        pe.wait_ge(free[B], count(i, 2, FREE_B["att"] + 1))
                        pe.wait_ge(free[C], count(i, 2, FREE_C["att"]))
                        for b in range(2):
                            for qs, keys, dst in ((slice(0, P), slice(0, K0), slice(0, K0)),
                                                  (slice(P, 2 * P), slice(0, TOK), slice(K0, SC))):
                                last = product(ps[:, C + b, dst], q_hi[:, b, qs], q_lo[:, b, qs],
                                               k_hi[:, b, keys], k_lo[:, b, keys])
                        last.then_inc(s_done, 1)
                    if j == 12:
                        pe.wait_ge(free[A], count(i, 2, FREE_A["att"] + 2))
                        pe.wait_ge(free[E], count(i, 2, FREE_E["att"]))
                        for b in range(2):
                            for t in range(3):
                                toks = slice(t * P, min((t + 1) * P, TOK))
                                last = nc.tensor.transpose(ps[0:toks.stop - toks.start, E + b, t * P:(t + 1) * P],
                                                           v_t[:, b, toks], ident[:])
                        last.then_inc(v_turned, 1)
                    if j == 13:
                        pe.wait_ge(att_step, count(i, ATT_STEPS, 4))
                        pe.wait_ge(free[C], count(i, 2, FREE_C["att"] + 1))
                        for b in range(2):
                            nc.tensor.transpose(ps[:, C + b, 0:P], probs[:, b, 0:P], ident[:])
                            nc.tensor.transpose(ps[:, C + b, P:2 * P], probs[:, b, K0:K0 + P], ident[:])
                            nc.tensor.transpose(ps[:, C + b, 2 * P:3 * P], probs[:, b, K0 + P:K0 + 2 * P], ident[:])
                            for t, keys in enumerate((slice(P, K0), slice(SC - META, SC))):
                                tail = slice(3 * P + t * META, 3 * P + (t + 1) * META)
                                last = nc.tensor.matmul(ps[0:META, C + b, tail], probs[:, b, keys],
                                                        ident[:, P - META:P], start=True, stop=True)
                        last.then_inc(p_turned, 1)
                pe.wait_ge(free[C], count(i, 2, FREE_C["att"] + 2))
                pe.wait_ge(free[E], count(i, 2, FREE_E["att"] + 1))
                for b in range(2):
                    o = ps[:, E + b, 0:SEQ]
                    product(o, v_hi[:, b, 0:P], v_lo[:, b, 0:P], p_hi[:, b, 0:2 * P], p_lo[:, b, 0:2 * P],
                            stop=False)
                    first, second = slice(0, META), slice(META, 2 * META)
                    product(o[:, P - META:P], v_hi[0:META, b, P:2 * P], v_lo[0:META, b, P:2 * P],
                            tail_hi[:, b, first], tail_lo[:, b, first], start=False, stop=False)
                    product(o[:, P:2 * P], v_hi[:, b, P:2 * P], v_lo[:, b, P:2 * P],
                            p_hi[:, b, 2 * P:3 * P], p_lo[:, b, 2 * P:3 * P], start=False, stop=False)
                    last = product(o[:, 2 * P - META:2 * P], v_hi[0:META, b, 2 * P:3 * P],
                                   v_lo[0:META, b, 2 * P:3 * P], tail_hi[:, b, second], tail_lo[:, b, second],
                                   start=False)
                last.then_inc(pv_done, 1)

            with pe.Fori(0, PAIRS) as i:
                for j in range(N_MERGE):
                    bank = (A, B)[j // PER]
                    if j % PER == 0:
                        pe.wait_ge(free[bank], count(i, 1, FREE_A["ma"]))
                    if j == PER:
                        pe.wait_ge(o_split, 2 * PAIRS)
                    src_hi, src_lo, part = (h_hi, h_lo, REAL) if j < PER else (o_hi, o_lo, slice(0, SEQ))
                    project(i, N_MERGE, U_MA + j, bank, src_hi, src_lo, part, j % PER * UK)

            def out_product(u, t, q):
                k, c = u // OUT_STEP * OUT_K + u % OUT_K, u // OUT_K % 2
                toks, w, slot = slice(t * P, (t + 1) * P), slice(q * HALF, (q + 1) * HALF), (U_OUT + u) % RING
                last = product(ps[:, OUT_BANK[c] + 2 * t + q, :], m_hi[:, k, toks], m_lo[:, k, toks],
                               w_hi[:, slot, w], w_lo[:, slot, w], start=(k == 0), stop=(k == KT - 1))
                if k == KT - 1:
                    last.then_inc(y_ready, 1)
                return last

            for u in range(N_OUT - RING):
                k, c = u // OUT_STEP * OUT_K + u % OUT_K, u // OUT_K % 2
                if k == 0:
                    for bank, name in (((C, FREE_C), (E, FREE_E)), ((A, FREE_A), (B, FREE_B)))[c]:
                        pe.wait_ge(free[bank], name["out"])
                if c == 0 and k % 2 == 0:
                    pe.wait_ge(m_split, k // 2 + 1)
                pe.wait_ge(w_split, RAW + U_OUT + u + 1)
                for t in range(2):
                    for q in range(2):
                        last = out_product(u, t, q)
                last.then_inc(w_used, 1)
            last_units = list(range(N_OUT - RING, N_OUT))
            pe.wait_ge(m_split, PAIRS)
            for u in last_units:
                pe.wait_ge(w_split, RAW + U_OUT + u + 1)
                for q in range(2):
                    out_product(u, 0, q)
            for u in last_units[:OUT_K]:
                for q in range(2):
                    out_product(u, 1, q)
            for q in range(2):
                for u in last_units[OUT_K:]:
                    out_product(u, 1, q)


_INS = ["x", "meta_tokens", "norm_gain", "w_in", "b_f", "conv_w", "w_att_o", "w_conv_o", "w_out", "final_gain"]


def kernel(**inputs):
    import numpy as np
    import concourse.bacc as bacc
    from concourse.bass_utils import run_bass_kernel_spmd

    nc = bacc.Bacc("TRN2", target_bir_lowering=False, num_devices=1)
    arrays, args = {}, []
    for name in _INS:
        a = np.ascontiguousarray(inputs[name])
        if name in ("x", "w_in", "conv_w", "w_att_o", "w_conv_o", "w_out"):
            a = a.reshape(a.shape[1:])
        arrays[f"in_{name}"] = a
        args.append(nc.dram_tensor(f"in_{name}", a.shape, mybir.dt.from_np(a.dtype), kind="ExternalInput").ap())
    neg_c_dram = nc.dram_tensor("neg_c_dram", (HEADS, TOK), F32, kind="Internal").ap()
    out = nc.dram_tensor("out", (SEQ, D), F32, kind="ExternalOutput").ap()
    hybrid_block(nc, *args, neg_c_dram, out)
    r = run_bass_kernel_spmd(nc, [arrays], core_ids=[0])
    return r.results[0]["out"].reshape(1, SEQ, D)
```

```python
from contextlib import ExitStack

import concourse.bass as bass
from concourse import mybir

F32 = mybir.dt.float32
F32R = mybir.dt.float32r
ALU = mybir.AluOpType
ACT = mybir.ActivationFunctionType
AX = mybir.AxisListType

P = 128
D = 2048
SEQ = 256
META = 16
TOK = META + SEQ
HEADS = 16
DH = 128
TAPS = 3
EPS = 1e-6
SCALE = DH ** -0.5
NEG = -1e30

KT = D // P
PAIRS = KT // 2
CONV_TOK = SEQ + TAPS - 1

COL_Q, COL_K, COL_V, COL_F = 0, D, 2 * D, 3 * D
COL_Z = COL_F + HEADS
COL_U, COL_GB, COL_GC, COL_ZC = COL_Z + D, COL_Z + 2 * D, COL_Z + 3 * D, COL_Z + 4 * D
COL_MA, COL_MC = COL_Z + 5 * D, COL_Z + 6 * D

UNIT = 1024
RAW, RING, LEAD = 4, 8, 5
UK = 4
PER = KT // UK
N_CONV, N_F, N_MERGE, N_ATT, N_OUT = 4 * PER, 2, 2 * PER, 4 * PER, 2 * KT
U_CONV = 0
U_F = U_CONV + N_CONV * PAIRS
U_MC = U_F + N_F
U_ATT = U_MC + N_MERGE * PAIRS
U_MA = U_ATT + N_ATT * PAIRS
U_OUT = U_MA + N_MERGE * PAIRS
UNITS = U_OUT + N_OUT
OUT_STEP = 8
OUT_K = OUT_STEP // 2
HALF = 512

K0 = META + P
SC = K0 + TOK
TAIL = 2 * META

HI, LO = 0, 1

OUT_BANK = (4, 0)
A, B, C, E = 0, 2, 4, 6
FREE_A = {"conv": 1, "mc": 1 + PAIRS, "att": 1 + 2 * PAIRS, "ma": 1 + 4 * PAIRS, "out": 1 + 5 * PAIRS}
FREE_B = FREE_A
FREE_C = {"conv": 1, "f": 1 + PAIRS, "att": 2 + PAIRS, "out": 2 + 3 * PAIRS}
FREE_E = {"conv": 1, "att": 1 + PAIRS, "out": 1 + 3 * PAIRS}


def hybrid_block(nc, x, meta_tokens, norm_gain, w_in, b_f, conv_w, w_att_o, w_conv_o, w_out,
                 final_gain, neg_c_dram, out):
    at, end = {}, {}
    base = (nc.sbuf_base + 31) // 32 * 32

    def region(name, size):
        nonlocal base
        at[name] = base
        base += size
        end[name] = base

    region("h", 2 * KT * TOK * 4)
    region("o", 2 * KT * SEQ * 4)
    region("p", KT * SEQ * 4)
    region("m", 2 * KT * SEQ * 4)
    region("raw", RAW * UNIT * 4)
    region("hi", RING * UNIT * 4)
    region("lo", RING * UNIT * 4)
    region("misc", 13 * 1024)

    def place(reg, name, shape, dtype=F32):
        t = nc.alloc_sbuf_tensor_at(name, shape, dtype, offset=at[reg])
        size = 4
        for s in shape[1:]:
            size *= s
        at[reg] += (size + 31) // 32 * 32
        assert at[reg] <= end[reg], name
        return t

    misc = lambda name, shape, dtype=F32: place("misc", name, shape, dtype)
    ident = misc("ident", [P, P])
    chan_rows = misc("chan_rows", [(TAPS + 1) * KT, P])
    chan = misc("chan", [P, TAPS + 1, KT])
    bf = misc("bf", [HEADS, 1])
    mask = misc("mask", [P, SC])
    gate = misc("gate", [P, 2, SEQ])
    prod = misc("prod", [P, 2, SEQ])
    prod2 = misc("prod2", [P, 2, SEQ])
    joined = misc("joined", [P, 2, SEQ])
    tail_row = misc("tail_row", [2 * META, 2])
    sumsq = misc("sumsq", [P, 2, 2])
    sums = misc("sums", [P, 2])
    warm_up = misc("warm_up", [P, 4])
    meta_sumsq = misc("meta_sumsq", [META, 1])
    y_sumsq = misc("y_sumsq", [P, 8])
    y_mean = misc("y_mean", [P, 8])
    var = misc("var", [P, 4])
    minus_half = misc("minus_half", [P, 4])
    rstd = misc("rstd", [P, 4])
    nmax = misc("nmax", [P, 2, 2])
    smax = misc("smax", [P, 2, 2])
    den = misc("den", [P, 2, 2])
    rden = misc("rden", [P, 2, 2])

    w_raw = place("raw", "w_raw", [P, RAW, UNIT])
    w_hi = place("hi", "w_hi", [P, RING, UNIT], F32R)
    w_lo = place("lo", "w_lo", [P, RING, UNIT], F32R)

    h_at, o_at, m_at = at["h"], at["o"], at["m"]
    x_nat = place("o", "x_nat", [P, 2, D])
    meta_nat = place("o", "meta_nat", [META, D])
    square = place("m", "square", [P, 2, D])
    p_at = at["p"]
    square_meta = place("p", "square_meta", [META, D])
    at["o"], at["m"], at["p"] = o_at, m_at, p_at
    h = place("h", "h", [P, 2, KT, TOK], F32R)
    o = place("o", "o", [P, 2, KT, SEQ], F32R)
    partial = place("p", "partial", [P, KT, SEQ])
    u_sb = place("m", "u_sb", [P, 2, CONV_TOK])
    cu = place("m", "cu", [P, 2, CONV_TOK])
    conv = [place("m", f"conv{j}", [P, 2, SEQ]) for j in range(TAPS)]
    conv_gated = place("m", "conv_gated", [P, 2, SEQ])
    at["m"] = m_at
    f_x = place("m", "f_x", [HEADS, TOK])
    f_na = place("m", "f_na", [HEADS, TOK])
    f_e = place("m", "f_e", [HEADS, TOK])
    f_l = place("m", "f_l", [HEADS, TOK])
    f_mn = place("m", "f_mn", [HEADS, TOK])
    f_nlog = place("m", "f_nlog", [HEADS, TOK])
    f_one = place("m", "f_one", [HEADS, TOK])
    neg_c = place("m", "neg_c", [HEADS, TOK])
    at["m"] = m_at
    neg_cb = place("m", "neg_cb", [P, 2, TOK])
    bias = place("m", "bias", [P, 2, SC])
    k_hi = place("m", "k_hi", [P, 2, TOK], F32R)
    k_lo = place("m", "k_lo", [P, 2, TOK], F32R)
    q_hi = place("m", "q_hi", [P, 2, SEQ], F32R)
    q_lo = place("m", "q_lo", [P, 2, SEQ], F32R)
    v_t = place("m", "v_t", [P, 2, 2 * P])
    v_hi = place("m", "v_hi", [P, 2, 2 * P], F32R)
    v_lo = place("m", "v_lo", [P, 2, 2 * P], F32R)
    probs = place("m", "probs", [P, 2, SC])
    probs_t = place("m", "probs_t", [P, 2, 2, 3 * P], F32R)
    v_tail_t = place("m", "v_tail_t", [P, 2, 2, META])
    probs_tail = place("m", "probs_tail", [P, 2, 2, META])
    v_tail = place("m", "v_tail", [3 * TAIL, 2, P], F32R)
    p_tail = place("m", "p_tail", [3 * TAIL, 2, 2, META], F32R)
    at["m"] = m_at
    m_hi = place("m", "m_hi", [P, KT, SEQ], F32R)
    m_lo = place("m", "m_lo", [P, KT, SEQ], F32R)
    at["h"], at["o"], at["p"] = h_at, o_at, p_at
    x_res = place("h", "x_res", [P, 2, D])
    gain_b = place("h", "gain_b", [P, D])
    y = place("o", "y", [P, 2, D])
    square2 = place("o", "square2", [P, 2, D])
    y_gain = place("p", "y_gain", [P, 2, D])
    assert base <= nc.sbuf_usable_end

    with ExitStack() as ctx:
        ps = ctx.enter_context(nc.psum_tensor("ps", [P, 8, 512], F32))
        sem = lambda name: ctx.enter_context(nc.semaphore(name))

        x_landed = [[sem(f"x_landed{t}{c}") for c in range(2)] for t in range(2)]
        meta_landed = sem("meta_landed")
        warm = sem("warm")
        rows_landed = sem("rows_landed")
        bf_landed = sem("bf_landed")
        w_landed = [sem(f"w_landed{s}") for s in range(RAW)]
        w_rounded = sem("w_rounded")
        w_split = sem("w_split")
        w_used = sem("w_used")
        w_first = sem("w_first")
        free = {A: sem("free_a"), B: sem("free_b"), C: sem("free_c"), E: sem("free_e")}
        consts = sem("consts")
        ones_made = sem("ones_made")
        ss_act, ss_dve = sem("ss_act"), sem("ss_dve")
        var_done, rstd_done = sem("var_done"), sem("rstd_done")
        normed = [sem(f"normed{t}") for t in range(3)]
        last_normed = sem("last_normed")
        chan_t, chan_done = sem("chan_t"), sem("chan_done")
        h_turned, h_rounded, h_split = sem("h_turned"), sem("h_rounded"), sem("h_split")
        conv_step, conv_sig = sem("conv_step"), sem("conv_sig")
        o_rounded, o_split = sem("o_rounded"), sem("o_split")
        f_dve, f_act, c_stored = sem("f_dve"), sem("f_act"), sem("c_stored")
        bias_landed, bias_made = sem("bias_landed"), sem("bias_made")
        q_split, gate_ready, mc_step = sem("q_split"), sem("gate_ready"), sem("mc_step")
        kq_rounded, v_rounded, p_rounded = sem("kq_rounded"), sem("v_rounded"), sem("p_rounded")
        s_done, exp_done, v_turned, p_turned, pv_done = (
            sem("s_done"), sem("exp_done"), sem("v_turned"), sem("p_turned"), sem("pv_done"))
        att_step, z_exp = sem("att_step"), sem("z_exp")
        merge_step, m_rounded, m_split = sem("merge_step"), sem("m_rounded"), sem("m_split")
        y_ready = sem("y_ready")
        x_res_landed, gain_landed = sem("x_res_landed"), sem("gain_landed")
        y_added, y_ss, y_gained, y_var, y_rstd = (
            sem("y_added"), sem("y_ss"), sem("y_gained"), sem("y_var"), sem("y_rstd"))
        y_scaled = [sem("y_scaled_left"), sem("y_scaled_right")]
        stored = sem("stored")

        block = ctx.enter_context(nc.Block())

        CONV_STEPS = 6
        ATT_STEPS = 9
        MERGE_STEPS = 2

        Y_PIECES = [(0, slice(0, UNIT)), (0, slice(UNIT, D)),
                    (1, slice(0, UNIT)), (1, slice(UNIT, UNIT + HALF)), (1, slice(UNIT + HALF, D))]
        Y_READY = (2, 4, 6, 7, 8)
        Y_LAST = (1, 4)

        def h_bank(k):
            return 2 + k % 6

        def count(i, per, c):
            return c if i is None else i * per + c

        @block.sync
        def _(sp):
            def load(i, per, c, src, k=UK):
                sp.wait_ge(w_split, count(i, per, c + 1))
                dst = w_raw[:, c % RAW, :].rearrange("p (k n) -> p k n", k=k)
                sp.dma_start(dst, src).then_inc(w_landed[c % RAW], 16)

            def load_stage(first, sources):
                per = PER * len(sources)
                with sp.Fori(1, PAIRS + 1) as i:
                    for j in range(per):
                        w_k, col = sources[j // PER]
                        rows = slice(j % PER * UK, j % PER * UK + UK)
                        load(i, per, first + j - per,
                             w_k[:, rows, bass.ds(i * (2 * P) + (col - 2 * P), 2 * P)])

            w_in_k, w_conv_k, w_att_k, w_out_k = (
                w.rearrange("(k p) n -> p k n", p=P) for w in (w_in, w_conv_o, w_att_o, w_out))
            for t in range(2):
                for c in range(2):
                    cols = slice(c * D // 2, (c + 1) * D // 2)
                    sp.dma_start(x_nat[:, t, cols], x[t * P:(t + 1) * P, cols]).then_inc(x_landed[t][c], 16)
            sp.dma_start(chan_rows[0:TAPS * KT, :], conv_w.rearrange("t (k p) -> (t k) p", p=P)
                         ).then_inc(rows_landed, 16)
            sp.dma_start(chan_rows[TAPS * KT:(TAPS + 1) * KT, :], norm_gain.rearrange("a (k p) -> (a k) p", p=P)
                         ).then_inc(rows_landed, 16)
            sp.dma_start(bf[:], b_f.rearrange("a h -> h a")).then_inc(bf_landed, 16)
            load_stage(U_CONV, [(w_in_k, COL_U), (w_in_k, COL_GC), (w_in_k, COL_GB), (w_in_k, COL_ZC)])
            for j in range(N_F):
                load(None, 0, U_F + j, w_in_k[:, j * 8:j * 8 + 8, COL_F:COL_F + P], k=8)
            load_stage(U_MC, [(w_in_k, COL_MC), (w_conv_k, 0)])
            load_stage(U_ATT, [(w_in_k, COL_K), (w_in_k, COL_Q), (w_in_k, COL_V), (w_in_k, COL_Z)])
            load_stage(U_MA, [(w_in_k, COL_MA), (w_att_k, 0)])
            with sp.Fori(0, N_OUT // OUT_STEP) as i:
                for j in range(OUT_STEP):
                    half = slice(j // OUT_K * UNIT, (j // OUT_K + 1) * UNIT)
                    load(i, OUT_STEP, U_OUT + j, w_out_k[:, bass.ds(i * OUT_K + j % OUT_K, 1), half], k=1)
            sp.wait_ge(w_used, RING + U_OUT)
            sp.dma_start(x_res[:], x.rearrange("(t p) d -> p t d", p=P)).then_inc(x_res_landed, 16)
            sp.dma_start(gain_b[:], final_gain.partition_broadcast(P)).then_inc(gain_landed, 16)
            for t in range(2):
                for n in range(2):
                    for side in (1, 0):
                        cols = slice(side * UNIT + n * HALF, side * UNIT + (n + 1) * HALF)
                        sp.wait_ge(y_scaled[side], 2 * t + n + 1)
                        sp.dma_start(out[t * P:(t + 1) * P, cols], y[:, t, cols]).then_inc(stored, 16)
            sp.wait_ge(stored, 8 * 16)

        @block.gpsimd
        def _(pool):
            nc.gpsimd.memset(ident[:], 1.0).then_inc(ones_made, 1)
            nc.gpsimd.memset(mask[:], 0.0).then_inc(ones_made, 1)
            nc.gpsimd.memset(minus_half[:], -0.5).then_inc(ones_made, 1)
            nc.gpsimd.memset(tail_row[:], 1.0).then_inc(ones_made, 1)
            pool.wait_ge(ones_made, 4)
            nc.gpsimd.affine_select(out=ident[:], in_=ident[:], pattern=[[-1, P]], compare_op=ALU.is_equal,
                                    fill=0.0, base=0, channel_multiplier=1).then_inc(consts, 1)
            nc.gpsimd.affine_select(out=tail_row[:, 0:1], in_=tail_row[:, 0:1], pattern=[[1, 1]],
                                    compare_op=ALU.is_ge, fill=0.0, base=META - 1, channel_multiplier=-1)
            nc.gpsimd.affine_select(out=tail_row[:, 1:2], in_=tail_row[:, 1:2], pattern=[[1, 1]],
                                    compare_op=ALU.is_ge, fill=0.0, base=-META, channel_multiplier=1)
            nc.gpsimd.affine_select(out=mask[:, 0:K0], in_=mask[:, 0:K0], pattern=[[-1, K0]],
                                    compare_op=ALU.is_ge, fill=NEG, base=META, channel_multiplier=1)
            nc.gpsimd.affine_select(out=mask[:, K0:SC], in_=mask[:, K0:SC], pattern=[[-1, TOK]],
                                    compare_op=ALU.is_ge, fill=NEG, base=K0, channel_multiplier=1
                                    ).then_inc(consts, 1)
            for n, (t, rows) in enumerate(((0, P), (2, META), (1, P))):
                pool.wait_ge(var_done, n + 1)
                nc.gpsimd.tensor_tensor(rstd[0:rows, t:t + 1], var[0:rows, t:t + 1], minus_half[0:rows, t:t + 1],
                                        ALU.pow).then_inc(rstd_done, 1)
            pool.wait_ge(consts, 2)
            pool.sem_inc(bias_made, 1)
            with pool.Fori(0, PAIRS) as i:
                pool.wait_ge(bias_landed, i * 16 + 16)
                pool.wait_ge(free[C], i * 2 + FREE_C["att"])
                for b in range(2):
                    nc.gpsimd.tensor_tensor(bias[:, b, 0:K0], mask[:, 0:K0], neg_cb[:, b, 0:K0], ALU.add)
                    last = nc.gpsimd.tensor_tensor(bias[:, b, K0:SC], mask[:, K0:SC], neg_cb[:, b, :], ALU.add)
                last.then_inc(bias_made, 1)
            for t, n in enumerate(Y_LAST):
                pool.wait_ge(y_var, n + 1)
                nc.gpsimd.tensor_tensor(rstd[:, t:t + 1], y_mean[:, n:n + 1], minus_half[:, t:t + 1],
                                        ALU.pow).then_inc(y_rstd, 1)

        @block.scalar
        def _(act):
            def round_unit(i, per, c):
                act.wait_ge(w_landed[c % RAW], count(i, per // RAW * 16, c // RAW * 16 + 16))
                act.wait_ge(w_used, count(i, per, c + 1))
                nc.scalar.copy(w_hi[:, c % RING, :], w_raw[:, c % RAW, :]).then_inc(w_rounded, 1)

            act.dma_start(meta_nat[:], meta_tokens).then_inc(meta_landed, 16)
            act.wait_ge(ones_made, 3)
            nc.scalar.activation(warm_up[:], minus_half[:], ACT.Square).then_inc(warm, 1)
            for t in range(2):
                for c in range(2):
                    cols = slice(c * D // 2, (c + 1) * D // 2)
                    act.wait_ge(x_landed[t][c], 16)
                    nc.scalar.activation(square[:, t, cols], x_nat[:, t, cols], ACT.Square,
                                         accum_out=sumsq[:, t, c:c + 1]).then_inc(ss_act, 1)
            act.wait_ge(chan_t, 1)
            nc.scalar.copy(chan[:], ps[:, 0, 0:(TAPS + 1) * KT].rearrange("p (t k) -> p t k", k=KT)
                           ).then_inc(chan_done, 1)
            round_unit(None, 0, 0)
            act.wait_ge(rstd_done, 3)
            last_quarter = slice(3 * D // 4, D)
            nc.scalar.activation(x_nat[:, 1, last_quarter], x_nat[:, 1, last_quarter], ACT.Copy,
                                 scale=rstd[:, 1:2]).then_inc(last_normed, 1)
            act.wait_ge(chan_done, 1)
            for k in range(KT):
                act.wait_ge(h_turned, k + 1)
                nc.scalar.activation(h[:, HI, k, :], ps[:, h_bank(k), 0:TOK], ACT.Copy,
                                     scale=chan[:, TAPS, k:k + 1]).then_inc(h_rounded, 1)
                if k % 3 == 0 and k > 0:
                    round_unit(None, 0, k // 3)
            for n in range(KT // 3 + 1, LEAD + 1):
                round_unit(None, 0, n)

            with act.Fori(0, PAIRS) as i:
                for j in range(1, N_CONV + 1):
                    round_unit(i, N_CONV, U_CONV + j + LEAD)
                    if j == PER:
                        act.wait_ge(w_used, count(i, N_CONV, RING + U_CONV + j))
                        nc.scalar.copy(u_sb[:], ps[:, A:A + 2, 0:CONV_TOK]).then_inc(free[A], 1)
                act.wait_ge(free[E], count(i, 1, FREE_E["conv"] + 1))
                nc.scalar.activation(gate[:], joined[:], ACT.Sigmoid).then_inc(conv_sig, 1)
                act.wait_ge(conv_step, count(i, CONV_STEPS, 6))
                nc.scalar.copy(o[:, HI, bass.ds(i * 2, 2), :], prod2[:]).then_inc(o_rounded, 1)

            for j in range(1, N_F + 1):
                round_unit(None, 0, U_F + j + LEAD)
            act.wait_ge(f_dve, 1)
            nc.scalar.activation(f_e[:], f_na[:], ACT.Exp).then_inc(f_act, 1)
            act.wait_ge(f_act, 1)
            nc.scalar.activation(f_l[:], f_e[:], ACT.Ln, bias=1.0).then_inc(f_act, 1)
            act.wait_ge(f_dve, 4)
            act.dma_start(neg_c_dram, neg_c[:]).then_inc(c_stored, 16)

            with act.Fori(0, PAIRS) as i:
                for j in range(1, N_MERGE + 1):
                    round_unit(i, N_MERGE, U_MC + j + LEAD)
                    if j == PER:
                        act.wait_ge(free[A], count(i, 1, FREE_A["mc"] + 1))
                        nc.scalar.activation(gate[:], prod[:], ACT.Sigmoid).then_inc(gate_ready, 1)

            act.wait_ge(c_stored, 16)
            with act.Fori(0, PAIRS) as i:
                for j in range(1, N_ATT + 1):
                    round_unit(i, N_ATT, U_ATT + j + LEAD)
                    if j == 2:
                        act.wait_ge(bias_made, count(i, 1, 1))
                        act.dma_start(neg_cb[:], neg_c_dram[bass.ds(i * 2, 2), :].partition_broadcast(P)
                                      ).then_inc(bias_landed, 16)
                    if j in (PER, 2 * PER, 3 * PER):
                        if j == 2 * PER:
                            act.wait_ge(free[B], count(i, 2, FREE_B["att"] + 1))
                        else:
                            act.wait_ge(w_used, count(i, N_ATT, RING + U_ATT + j))
                        if j == PER:
                            nc.scalar.copy(k_hi[:], ps[:, A:A + 2, 0:TOK]).then_inc(kq_rounded, 1)
                        elif j == 2 * PER:
                            nc.scalar.copy(q_hi[:], joined[:]).then_inc(kq_rounded, 1)
                        else:
                            nc.scalar.copy(v_t[:], ps[:, A:A + 2, 0:2 * P])
                            nc.scalar.copy(v_tail_t[:], ps[:, A:A + 2, META:TOK].rearrange(
                                "p b (t n) -> p b t n", n=P)[:, :, :, P - META:P]).then_inc(free[A], 1)
                    if j == 11:
                        act.wait_ge(att_step, count(i, ATT_STEPS, 2))
                        for b in range(2):
                            for t, keys in enumerate((slice(0, K0), slice(K0, SC))):
                                last = nc.scalar.activation(probs[:, b, keys], probs[:, b, keys], ACT.Exp,
                                                            bias=nmax[:, b, t:t + 1],
                                                            accum_out=den[:, b, t:t + 1])
                        last.then_inc(exp_done, 1)
                    if j == 14:
                        act.wait_ge(v_turned, count(i, 1, 1))
                        nc.scalar.copy(v_hi[:], ps[:, E:E + 2, 0:2 * P])
                        for rows in (slice(0, TAIL), slice(TAIL, 2 * TAIL)):
                            last = nc.scalar.copy(v_tail[rows, :, :], ps[0:TAIL, E:E + 2, 2 * P:3 * P])
                        last.then_inc(v_rounded, 1)
                    if j == 15:
                        act.wait_ge(p_turned, count(i, 1, 1))
                        nc.scalar.copy(probs_t[:, HI, :, :], ps[:, C:C + 2, 0:3 * P])
                        for rows in (slice(0, TAIL), slice(2 * TAIL, 3 * TAIL)):
                            for t in range(2):
                                last = nc.scalar.activation(p_tail[rows, :, t, :],
                                                            ps[0:TAIL, C:C + 2, 3 * P:3 * P + META],
                                                            ACT.Copy, scale=tail_row[:, t:t + 1])
                        last.then_inc(p_rounded, 1)
                act.wait_ge(free[B], count(i, 2, FREE_B["att"] + 2))
                nc.scalar.activation(gate[:], joined[:], ACT.Exp, scale=-1.0).then_inc(z_exp, 1)
                act.wait_ge(att_step, count(i, ATT_STEPS, ATT_STEPS))
                nc.scalar.copy(o[:, HI, bass.ds(i * 2, 2), :], prod2[:]).then_inc(o_rounded, 1)

            with act.Fori(0, PAIRS) as i:
                for j in range(1, N_MERGE + 1):
                    round_unit(i, N_MERGE, U_MA + j + LEAD)
                    if j == PER:
                        act.wait_ge(free[A], count(i, 1, FREE_A["ma"] + 1))
                        nc.scalar.activation(gate[:], prod[:], ACT.Sigmoid).then_inc(gate_ready, 1)
                act.wait_ge(merge_step, count(i, MERGE_STEPS, 2))
                nc.scalar.copy(m_hi[:, bass.ds(i * 2, 2), :], prod2[:]).then_inc(m_rounded, 1)

            rest = UNITS - (U_OUT + 1 + LEAD)
            with act.Fori(0, rest // RING) as i:
                for j in range(RING):
                    round_unit(i, RING, U_OUT + 1 + LEAD + j)
            for n in range(UNITS - rest % RING, UNITS):
                round_unit(None, 0, n)
            for n, (t, cols) in enumerate(Y_PIECES):
                act.wait_ge(y_added, n + 1)
                nc.scalar.activation(square2[:, t, cols], y[:, t, cols], ACT.Square,
                                     accum_out=y_sumsq[:, n:n + 1]).then_inc(y_ss, 1)
                if n in Y_LAST:
                    act.wait_ge(y_rstd, t + 1)
                    for cols in (slice(0, HALF), slice(HALF, UNIT)):
                        nc.scalar.activation(y[:, t, cols], y_gain[:, t, cols], ACT.Copy, scale=rstd[:, t:t + 1]
                                             ).then_inc(y_scaled[0], 1)

        @block.vector
        def _(dve):
            def split_unit(i, per, c):
                dve.wait_ge(w_rounded, count(i, per, c + 1))
                nc.vector.tensor_tensor(w_lo[:, c % RING, :], w_raw[:, c % RAW, :],
                                        w_hi[:, c % RING, :].bitcast(F32), ALU.subtract).then_inc(w_split, 1)

            def join(bank, dst):
                nc.vector.tensor_reduce(dst[:], ps[:, bank:bank + 2, :].rearrange("p b (s n) -> p b n s", n=SEQ),
                                        AX.X, ALU.add).then_inc(free[bank], 1)

            dve.sem_inc(w_split, RAW)
            dve.sem_inc(w_used, RING)
            dve.wait_ge(meta_landed, 16)
            nc.vector.tensor_tensor_reduce(out=square_meta[:], in0=meta_nat[:], in1=meta_nat[:], scale=1.0,
                                           scalar=0.0, op0=ALU.mult, op1=ALU.add,
                                           accum_out=meta_sumsq[:]).then_inc(ss_dve, 1)

            def mean_square(t):
                dve.wait_ge(ss_act, 2 * t + 2)
                nc.vector.tensor_tensor(sums[:, t:t + 1], sumsq[:, t, 0:1], sumsq[:, t, 1:2], ALU.add
                                        ).then_inc(ss_dve, 1)
                dve.wait_ge(ss_dve, t + 2)
                nc.vector.tensor_scalar(var[:, t:t + 1], sums[:, t:t + 1], 1.0 / D, EPS, ALU.mult,
                                        ALU.add).then_inc(var_done, 1)

            def normalise(t, c):
                cols = slice(c * D // 4, (c + 1) * D // 4)
                nc.vector.tensor_scalar(x_nat[:, t, cols], x_nat[:, t, cols], rstd[:, t:t + 1], None, ALU.mult
                                        ).then_inc(normed[t], 1)

            def normalise_meta(c):
                cols = slice(c * D // 2, (c + 1) * D // 2)
                nc.vector.tensor_scalar(meta_nat[:, cols], meta_nat[:, cols], rstd[0:META, 2:3], None, ALU.mult
                                        ).then_inc(normed[2], 1)

            mean_square(0)
            nc.vector.tensor_scalar(var[0:META, 2:3], meta_sumsq[:], 1.0 / D, EPS, ALU.mult,
                                    ALU.add).then_inc(var_done, 1)
            dve.wait_ge(rstd_done, 1)
            for c in range(4):
                normalise(0, c)
            dve.wait_ge(rstd_done, 2)
            normalise_meta(0)
            mean_square(1)
            normalise_meta(1)

            def split_first(k):
                dve.wait_ge(w_rounded, 1)
                w = slice(k * UNIT // UK, (k + 1) * UNIT // UK)
                nc.vector.tensor_tensor(w_lo[:, 0, w], w_raw[:, 0, w], w_hi[:, 0, w].bitcast(F32), ALU.subtract
                                        ).then_inc(w_split if k == UK - 1 else w_first, 1)

            def split_h(k):
                dve.wait_ge(h_rounded, k + 1)
                nc.vector.scalar_tensor_tensor(out=h[:, LO, k, :], in0=ps[:, h_bank(k), 0:TOK],
                                               scalar=chan[:, TAPS, k:k + 1], in1=h[:, HI, k, :].bitcast(F32),
                                               op0=ALU.mult, op1=ALU.subtract).then_inc(h_split, 1)

            dve.wait_ge(rstd_done, 3)
            normalise(1, 0)
            split_first(0)
            normalise(1, 1)
            normalise(1, 2)
            dve.wait_ge(chan_done, 1)
            split_h(0)
            for k in range(1, UK):
                split_first(k)
                split_h(k)
            for k in range(UK, KT):
                if k % 3 == 1:
                    split_unit(None, 0, k // 3)
                split_h(k)
            dve.wait_ge(h_split, KT)
            for bank in (A, B, C, E):
                dve.sem_inc(free[bank], 1)
            for n in range(KT // 3, LEAD + 1):
                split_unit(None, 0, n)

            with dve.Fori(0, PAIRS) as i:
                def step(n):
                    dve.wait_ge(conv_step, count(i, CONV_STEPS, n))

                for j in range(1, N_CONV + 1):
                    split_unit(i, N_CONV, U_CONV + j + LEAD)
                    if j == 2 * PER:
                        dve.wait_ge(w_used, count(i, N_CONV, RING + U_CONV + j))
                        dve.wait_ge(free[A], count(i, 1, FREE_A["conv"]))
                        nc.vector.tensor_tensor(cu[:], ps[:, B:B + 2, 0:CONV_TOK], u_sb[:], ALU.mult
                                                ).then_inc(free[B], 1)
                        dve.wait_ge(free[B], count(i, 1, FREE_B["conv"] + 1))
                        for tap in range(TAPS):
                            if tap > 0:
                                step(tap)
                            for b in range(2):
                                w = chan[:, tap, bass.ds(i * 2 + b, 1)]
                                shifted = cu[:, b, tap:tap + SEQ]
                                if tap == 0:
                                    last = nc.vector.tensor_scalar(conv[0][:, b, :], shifted, w, None, ALU.mult)
                                else:
                                    last = nc.vector.scalar_tensor_tensor(
                                        out=conv[tap][:, b, :], in0=shifted, scalar=w,
                                        in1=conv[tap - 1][:, b, :], op0=ALU.mult, op1=ALU.add)
                            last.then_inc(conv_step, 1)
                    if j == 3 * PER:
                        dve.wait_ge(w_used, count(i, N_CONV, RING + U_CONV + j))
                        join(C, joined)
                        dve.wait_ge(free[C], count(i, 1, FREE_C["conv"] + 1))
                        step(3)
                        nc.vector.tensor_tensor(conv_gated[:], joined[:], conv[TAPS - 1][:], ALU.mult
                                                ).then_inc(conv_step, 1)
                dve.wait_ge(w_used, count(i, N_CONV, RING + U_CONV + N_CONV))
                step(4)
                join(E, joined)
                dve.wait_ge(free[E], count(i, 1, FREE_E["conv"] + 1))
                dve.wait_ge(conv_sig, count(i, 1, 1))
                nc.vector.tensor_tensor(prod[:], joined[:], gate[:], ALU.mult).then_inc(conv_step, 1)
                step(5)
                nc.vector.tensor_tensor(prod2[:], prod[:], conv_gated[:], ALU.mult).then_inc(conv_step, 1)
                dve.wait_ge(o_rounded, count(i, 1, 1))
                nc.vector.tensor_tensor(o[:, LO, bass.ds(i * 2, 2), :], prod2[:],
                                        o[:, HI, bass.ds(i * 2, 2), :].bitcast(F32), ALU.subtract
                                        ).then_inc(o_split, 1)

            for j in range(1, N_F + 1):
                split_unit(None, 0, U_F + j + LEAD)
            dve.wait_ge(w_used, RING + U_F + N_F)
            dve.wait_ge(bf_landed, 16)
            nc.vector.tensor_scalar(f_x[:], ps[0:HEADS, C, 0:TOK], bf[:], None, ALU.add
                                    ).then_inc(free[C], 1)
            dve.wait_ge(free[C], FREE_C["f"] + 1)
            nc.vector.scalar_tensor_tensor(out=f_na[:], in0=f_x[:], scalar=-1.0, in1=f_x[:], op0=ALU.mult,
                                           op1=ALU.min).then_inc(f_dve, 1)
            nc.vector.memset(f_one[:], 1.0)
            nc.vector.tensor_scalar(f_mn[:], f_x[:], 0.0, None, ALU.min).then_inc(f_dve, 1)
            dve.wait_ge(f_dve, 2)
            dve.wait_ge(f_act, 2)
            nc.vector.tensor_tensor(f_nlog[:], f_l[:], f_mn[:], ALU.subtract).then_inc(f_dve, 1)
            dve.wait_ge(f_dve, 3)
            nc.vector.tensor_tensor_scan(out=neg_c[:], data0=f_one[:], data1=f_nlog[:], initial=0.0,
                                         op0=ALU.mult, op1=ALU.add).then_inc(f_dve, 1)

            with dve.Fori(0, PAIRS) as i:
                for j in range(1, N_MERGE + 1):
                    split_unit(i, N_MERGE, U_MC + j + LEAD)
                    if j == PER:
                        dve.wait_ge(w_used, count(i, N_MERGE, RING + U_MC + j))
                        join(A, prod)
                dve.wait_ge(w_used, count(i, N_MERGE, RING + U_MC + N_MERGE))
                dve.wait_ge(gate_ready, count(i, 1, 1))
                join(B, joined)
                dve.wait_ge(free[B], count(i, 1, FREE_B["mc"] + 1))
                nc.vector.tensor_tensor(partial[:, bass.ds(i * 2, 2), :], joined[:], gate[:], ALU.mult
                                        ).then_inc(mc_step, 1)

            with dve.Fori(0, PAIRS) as i:
                def step(n):
                    dve.wait_ge(att_step, count(i, ATT_STEPS, n))

                for j in range(1, N_ATT + 1):
                    split_unit(i, N_ATT, U_ATT + j + LEAD)
                    if j == PER:
                        dve.wait_ge(kq_rounded, count(i, 2, 1))
                        nc.vector.tensor_tensor(k_lo[:], ps[:, A:A + 2, 0:TOK], k_hi[:].bitcast(F32), ALU.subtract
                                                ).then_inc(free[A], 1)
                    if j == 2 * PER:
                        dve.wait_ge(w_used, count(i, N_ATT, RING + U_ATT + j))
                        join(B, joined)
                        dve.wait_ge(free[B], count(i, 2, FREE_B["att"] + 1))
                        dve.wait_ge(kq_rounded, count(i, 2, 2))
                        nc.vector.tensor_tensor(q_lo[:], joined[:], q_hi[:].bitcast(F32), ALU.subtract
                                                ).then_inc(q_split, 1)
                    if j == 14:
                        dve.wait_ge(v_rounded, count(i, 1, 1))
                        nc.vector.tensor_tensor(v_lo[:], ps[:, E:E + 2, 0:2 * P], v_hi[:].bitcast(F32), ALU.subtract)
                        nc.vector.tensor_tensor(v_tail[2 * TAIL:3 * TAIL, :, :], ps[0:TAIL, E:E + 2, 2 * P:3 * P],
                                                v_tail[0:TAIL, :, :].bitcast(F32), ALU.subtract
                                                ).then_inc(free[E], 1)
                    if j == 10:
                        dve.wait_ge(s_done, count(i, 1, 1))
                        dve.wait_ge(bias_made, count(i, 1, 2))
                        nc.vector.scalar_tensor_tensor(out=probs[:], in0=ps[:, C:C + 2, 0:SC], scalar=SCALE,
                                                       in1=bias[:], op0=ALU.mult, op1=ALU.add
                                                       ).then_inc(free[C], 1)
                        dve.wait_ge(free[C], count(i, 2, FREE_C["att"] + 1))
                        nc.vector.tensor_reduce(smax[:, :, 0], probs[:, :, 0:K0], AX.X, ALU.max)
                        nc.vector.tensor_reduce(smax[:, :, 1], probs[:, :, K0:SC], AX.X, ALU.max
                                                ).then_inc(att_step, 1)
                        step(1)
                        nc.vector.tensor_scalar(nmax[:], smax[:], -1.0, None, ALU.mult).then_inc(att_step, 1)
                    if j == 12:
                        dve.wait_ge(exp_done, count(i, 1, 1))
                        nc.vector.reciprocal(rden[:], den[:]).then_inc(att_step, 1)
                        step(3)
                        for b in range(2):
                            for t, stop in enumerate((K0, SC)):
                                last = nc.vector.tensor_scalar(probs_tail[:, b, t, :],
                                                               probs[:, b, stop - META:stop],
                                                               rden[:, b, t:t + 1], None, ALU.mult)
                        last.then_inc(att_step, 1)
                        step(4)
                        for b in range(2):
                            for t, keys in enumerate((slice(0, K0), slice(K0, SC))):
                                last = nc.vector.tensor_scalar(probs[:, b, keys], probs[:, b, keys],
                                                               rden[:, b, t:t + 1], None, ALU.mult)
                        last.then_inc(att_step, 1)
                    if j == 15:
                        dve.wait_ge(p_rounded, count(i, 1, 1))
                        nc.vector.tensor_tensor(probs_t[:, LO, :, :], ps[:, C:C + 2, 0:3 * P],
                                                probs_t[:, HI, :, :].bitcast(F32), ALU.subtract)
                        for t in range(2):
                            last = nc.vector.scalar_tensor_tensor(
                                out=p_tail[TAIL:2 * TAIL, :, t, :], in0=ps[0:TAIL, C:C + 2, 3 * P:3 * P + META],
                                scalar=tail_row[:, t:t + 1], in1=p_tail[0:TAIL, :, t, :].bitcast(F32),
                                op0=ALU.mult, op1=ALU.subtract)
                        last.then_inc(free[C], 1)
                dve.wait_ge(w_used, count(i, N_ATT, RING + U_ATT + N_ATT))
                join(B, joined)
                dve.wait_ge(z_exp, count(i, 1, 1))
                nc.vector.tensor_scalar(prod[:], gate[:], 1.0, None, ALU.add).then_inc(att_step, 1)
                step(6)
                nc.vector.reciprocal(prod2[:], prod[:]).then_inc(att_step, 1)
                step(7)
                dve.wait_ge(free[B], count(i, 2, FREE_B["att"] + 2))
                nc.vector.tensor_tensor(prod[:], joined[:], prod2[:], ALU.mult).then_inc(att_step, 1)
                dve.wait_ge(pv_done, count(i, 1, 1))
                step(8)
                join(E, joined)
                dve.wait_ge(free[E], count(i, 2, FREE_E["att"] + 2))
                nc.vector.tensor_tensor(prod2[:], joined[:], prod[:], ALU.mult).then_inc(att_step, 1)
                dve.wait_ge(o_rounded, count(i, 1, PAIRS + 1))
                nc.vector.tensor_tensor(o[:, LO, bass.ds(i * 2, 2), :], prod2[:],
                                        o[:, HI, bass.ds(i * 2, 2), :].bitcast(F32), ALU.subtract
                                        ).then_inc(o_split, 1)

            dve.wait_ge(mc_step, PAIRS)
            with dve.Fori(0, PAIRS) as i:
                for j in range(1, N_MERGE + 1):
                    split_unit(i, N_MERGE, U_MA + j + LEAD)
                    if j == PER:
                        dve.wait_ge(w_used, count(i, N_MERGE, RING + U_MA + j))
                        join(A, prod)
                dve.wait_ge(w_used, count(i, N_MERGE, RING + U_MA + N_MERGE))
                dve.wait_ge(gate_ready, count(i, 1, PAIRS + 1))
                join(B, joined)
                dve.wait_ge(free[B], count(i, 1, FREE_B["ma"] + 1))
                nc.vector.tensor_tensor(prod[:], joined[:], gate[:], ALU.mult).then_inc(merge_step, 1)
                dve.wait_ge(merge_step, count(i, MERGE_STEPS, 1))
                nc.vector.tensor_tensor(prod2[:], prod[:], partial[:, bass.ds(i * 2, 2), :], ALU.add
                                        ).then_inc(merge_step, 1)
                dve.wait_ge(m_rounded, count(i, 1, 1))
                nc.vector.tensor_tensor(m_lo[:, bass.ds(i * 2, 2), :], prod2[:],
                                        m_hi[:, bass.ds(i * 2, 2), :].bitcast(F32), ALU.subtract
                                        ).then_inc(m_split, 1)

            rest = UNITS - (U_OUT + 1 + LEAD)
            with dve.Fori(0, rest // RING) as i:
                for j in range(RING):
                    split_unit(i, RING, U_OUT + 1 + LEAD + j)
            for n in range(UNITS - rest % RING, UNITS):
                split_unit(None, 0, n)
            dve.wait_ge(x_res_landed, 16)
            dve.wait_ge(gain_landed, 16)

            for n, (t, cols) in enumerate(Y_PIECES):
                dve.wait_ge(y_ready, Y_READY[n])
                bank = OUT_BANK[cols.start // UNIT] + 2 * t + cols.start % UNIT // HALF
                banks = (cols.stop - cols.start) // HALF
                nc.vector.tensor_tensor(y[:, t, cols], ps[:, bank:bank + banks, :], x_res[:, t, cols], ALU.add
                                        ).then_inc(y_added, 1)
                dve.wait_ge(y_added, n + 1)
                nc.vector.tensor_tensor(y_gain[:, t, cols], y[:, t, cols], gain_b[:, cols], ALU.mult
                                        ).then_inc(y_gained, 1)
                dve.wait_ge(y_ss, n + 1)
                if n == 0 or n - 1 in Y_LAST:
                    last = nc.vector.tensor_scalar(y_mean[:, n:n + 1], y_sumsq[:, n:n + 1], 1.0 / D, EPS,
                                                   ALU.mult, ALU.add)
                else:
                    dve.wait_ge(y_var, n)
                    last = nc.vector.scalar_tensor_tensor(out=y_mean[:, n:n + 1], in0=y_sumsq[:, n:n + 1],
                                                          scalar=1.0 / D, in1=y_mean[:, n - 1:n],
                                                          op0=ALU.mult, op1=ALU.add)
                last.then_inc(y_var, 1)
                if n in Y_LAST:
                    dve.wait_ge(y_gained, n + 1)
                    dve.wait_ge(y_rstd, t + 1)
                    for cols in (slice(UNIT, UNIT + HALF), slice(UNIT + HALF, D)):
                        nc.vector.tensor_scalar(y[:, t, cols], y_gain[:, t, cols], rstd[:, t:t + 1], None,
                                                ALU.mult).then_inc(y_scaled[1], 1)

        @block.tensor
        def _(pe):
            def project(i, per, c, bank, src, part, kt0, blocks=2, k_in=UK,
                        before=None, after=None, first=False):
                if not first:
                    pe.wait_ge(w_split, count(i, per, RAW + c + 1))
                width = UNIT // k_in
                cols = part.stop - part.start
                for kk in range(k_in):
                    k = kt0 + kk
                    if first and kk < k_in - 1:
                        pe.wait_ge(w_first, kk + 1)
                    elif first:
                        pe.wait_ge(w_split, RAW + 1)
                    if before:
                        before(k)
                    for b in range(blocks):
                        w = slice(kk * width + b * P, kk * width + (b + 1) * P)
                        hi, lo = w_hi[:, c % RING, w], w_lo[:, c % RING, w]
                        if cols == SEQ:
                            last = wide_product(halves(bank + b), hi, lo, src[:, :, k, part],
                                                start=(k == 0), stop=(k == KT - 1))
                        else:
                            last = product(ps[:, bank + b, 0:cols], hi, lo, src[:, HI, k, part],
                                           src[:, LO, k, part], start=(k == 0), stop=(k == KT - 1))
                        if kk == k_in - 1 and b == blocks - 1:
                            last.then_inc(w_used, 1)
                    if after:
                        after(k)

            def product(dst, a_hi, a_lo, b_hi, b_lo, start=True, stop=True):
                nc.tensor.matmul(dst, a_hi, b_hi, start=start, stop=False)
                nc.tensor.matmul(dst, a_hi, b_lo, start=False, stop=False)
                return nc.tensor.matmul(dst, a_lo, b_hi, start=False, stop=stop)

            def halves(bank):
                return ps[:, bank, :].rearrange("p (s n) -> p s n", n=SEQ)

            def tails(ap):
                return ap.rearrange("p (t n) -> p t n", n=P)[:, :, P - META:P]

            def wide_product(dst, a_hi, a_lo, b, start=True, stop=True):
                nc.tensor.matmul(dst, a_hi, b, start=start, stop=False)
                return nc.tensor.matmul(dst[:, HI, :], a_lo, b[:, HI, :], start=False, stop=stop)

            ALL, REAL, CONV = slice(0, TOK), slice(META, TOK), slice(META - TAPS + 1, TOK)

            def keep_busy(n):
                for _ in range(n):
                    nc.tensor.transpose(ps[:, 1, 0:P], ident[:], ident[:])

            pe.wait_ge(consts, 1)
            pe.wait_ge(x_landed[0][1], 16)
            keep_busy(16)
            pe.wait_ge(rows_landed, 32)
            rows = (TAPS + 1) * KT
            nc.tensor.transpose(ps[:, 0, 0:rows], chan_rows[:], ident[0:rows, 0:rows]).then_inc(chan_t, 1)
            keep_busy(8)
            pe.wait_ge(chan_done, 1)

            AHEAD = 4

            def turn(k):
                if k >= 6:
                    pe.wait_ge(h_split, k - 5)
                ch = slice(k * P, (k + 1) * P)
                if k % 8 == 0:
                    pe.wait_ge(normed[2], k // 8 + 1)
                nc.tensor.transpose(ps[:, h_bank(k), 0:META], meta_nat[:, ch], ident[0:META, 0:META])
                for t in range(2):
                    if k == 12 and t == 1:
                        pe.wait_ge(last_normed, 1)
                    elif k % 4 == 0:
                        pe.wait_ge(normed[t], k // 4 + 1)
                    last = nc.tensor.transpose(ps[:, h_bank(k), META + t * P:META + (t + 1) * P],
                                               x_nat[:, t, ch], ident[:])
                last.then_inc(h_turned, 1)

            def conv_pair(i, first):
                for j in range(first, N_CONV):
                    bank = (A, B, C, E)[j // PER]
                    if j % PER == 0:
                        name = {A: FREE_A, B: FREE_B, C: FREE_C, E: FREE_E}[bank]
                        pe.wait_ge(free[bank], count(i, 1, name["conv"]))
                    part = CONV if j < 2 * PER else REAL
                    project(i, N_CONV, U_CONV + j, bank, h, part, j % PER * UK)

            for k in range(AHEAD):
                turn(k)
            for j in range(PER):
                def before(k):
                    pe.wait_ge(h_split, k + 1)

                def after(k):
                    if k + AHEAD < KT:
                        turn(k + AHEAD)

                project(None, 0, U_CONV + j, A, h, CONV, j * UK, before=before, after=after, first=(j == 0))
            conv_pair(None, PER)
            with pe.Fori(1, PAIRS) as i:
                conv_pair(i, 0)

            pe.wait_ge(free[C], FREE_C["f"])
            for j in range(N_F):
                project(None, 0, U_F + j, C, h, ALL, j * 8, blocks=1, k_in=8)

            with pe.Fori(0, PAIRS) as i:
                for j in range(N_MERGE):
                    bank = (A, B)[j // PER]
                    if j % PER == 0:
                        pe.wait_ge(free[bank], count(i, 1, FREE_A["mc"]))
                    if j == PER:
                        pe.wait_ge(o_split, PAIRS)
                    src, part = (h, REAL) if j < PER else (o, slice(0, SEQ))
                    project(i, N_MERGE, U_MC + j, bank, src, part, j % PER * UK)

            with pe.Fori(0, PAIRS) as i:
                for j in range(N_ATT):
                    bank = (A, B)[j // PER % 2]
                    if j % PER == 0:
                        pe.wait_ge(free[bank], count(i, 2, FREE_A["att"] + j // (2 * PER)))
                    part = REAL if j // PER in (1, 3) else ALL
                    project(i, N_ATT, U_ATT + j, bank, h, part, j % PER * UK)
                    if j == 9:
                        pe.wait_ge(q_split, count(i, 1, 1))
                        pe.wait_ge(free[C], count(i, 2, FREE_C["att"]))
                        for b in range(2):
                            for qs, keys, dst in ((slice(0, P), slice(0, K0), slice(0, K0)),
                                                  (slice(P, 2 * P), slice(0, TOK), slice(K0, SC))):
                                last = product(ps[:, C + b, dst], q_hi[:, b, qs], q_lo[:, b, qs],
                                               k_hi[:, b, keys], k_lo[:, b, keys])
                        last.then_inc(s_done, 1)
                    if j == 12:
                        pe.wait_ge(free[A], count(i, 2, FREE_A["att"] + 2))
                        pe.wait_ge(free[E], count(i, 2, FREE_E["att"]))
                        for b in range(2):
                            for t in range(2):
                                toks = slice(t * P, (t + 1) * P)
                                nc.tensor.transpose(ps[:, E + b, toks], v_t[:, b, toks], ident[:])
                            last = nc.tensor.transpose(ps[0:TAIL, E + b, 2 * P:3 * P],
                                                       v_tail_t[:, b, :, :], ident[:])
                        last.then_inc(v_turned, 1)
                    if j == 13:
                        pe.wait_ge(att_step, count(i, ATT_STEPS, 5))
                        pe.wait_ge(free[C], count(i, 2, FREE_C["att"] + 1))
                        for b in range(2):
                            nc.tensor.transpose(ps[:, C + b, 0:P], probs[:, b, 0:P], ident[:])
                            nc.tensor.transpose(ps[:, C + b, P:2 * P], probs[:, b, K0:K0 + P], ident[:])
                            nc.tensor.transpose(ps[:, C + b, 2 * P:3 * P], probs[:, b, K0 + P:K0 + 2 * P], ident[:])
                            last = nc.tensor.matmul(ps[0:TAIL, C + b, 3 * P:3 * P + META],
                                                    probs_tail[:, b, :, :],
                                                    ident[:, P - META:P], start=True, stop=True)
                        last.then_inc(p_turned, 1)
                pe.wait_ge(free[C], count(i, 2, FREE_C["att"] + 2))
                pe.wait_ge(free[E], count(i, 2, FREE_E["att"] + 1))
                for b in range(2):
                    o_t = halves(E + b)
                    wide_product(o_t, v_hi[:, b, 0:P], v_lo[:, b, 0:P], probs_t[:, :, b, 0:2 * P], stop=False)
                    wide_product(o_t[:, :, P:2 * P], v_hi[:, b, P:2 * P], v_lo[:, b, P:2 * P],
                                 probs_t[:, :, b, 2 * P:3 * P], start=False, stop=False)
                    last = nc.tensor.matmul(tails(o_t[:, HI, :]), v_tail[:, b, :], p_tail[:, b, :, :],
                                            start=False, stop=True)
                last.then_inc(pv_done, 1)

            with pe.Fori(0, PAIRS) as i:
                for j in range(N_MERGE):
                    bank = (A, B)[j // PER]
                    if j % PER == 0:
                        pe.wait_ge(free[bank], count(i, 1, FREE_A["ma"]))
                    if j == PER:
                        pe.wait_ge(o_split, 2 * PAIRS)
                    src, part = (h, REAL) if j < PER else (o, slice(0, SEQ))
                    project(i, N_MERGE, U_MA + j, bank, src, part, j % PER * UK)

            def out_product(u, t, q):
                k, c = u // OUT_STEP * OUT_K + u % OUT_K, u // OUT_K % 2
                toks, w, slot = slice(t * P, (t + 1) * P), slice(q * HALF, (q + 1) * HALF), (U_OUT + u) % RING
                last = product(ps[:, OUT_BANK[c] + 2 * t + q, :], m_hi[:, k, toks], m_lo[:, k, toks],
                               w_hi[:, slot, w], w_lo[:, slot, w], start=(k == 0), stop=(k == KT - 1))
                if k == KT - 1:
                    last.then_inc(y_ready, 1)
                return last

            for u in range(N_OUT - RING):
                k, c = u // OUT_STEP * OUT_K + u % OUT_K, u // OUT_K % 2
                if k == 0:
                    for bank, name in (((C, FREE_C), (E, FREE_E)), ((A, FREE_A), (B, FREE_B)))[c]:
                        pe.wait_ge(free[bank], name["out"])
                if c == 0 and k % 2 == 0:
                    pe.wait_ge(m_split, k // 2 + 1)
                pe.wait_ge(w_split, RAW + U_OUT + u + 1)
                for t in range(2):
                    for q in range(2):
                        last = out_product(u, t, q)
                last.then_inc(w_used, 1)
            last_units = list(range(N_OUT - RING, N_OUT))
            pe.wait_ge(m_split, PAIRS)
            for u in last_units:
                pe.wait_ge(w_split, RAW + U_OUT + u + 1)
                for q in range(2):
                    out_product(u, 0, q)
            for u in last_units[:OUT_K]:
                for q in range(2):
                    out_product(u, 1, q)
            for q in range(2):
                for u in last_units[OUT_K:]:
                    out_product(u, 1, q)


_INS = ["x", "meta_tokens", "norm_gain", "w_in", "b_f", "conv_w", "w_att_o", "w_conv_o", "w_out", "final_gain"]


def kernel(**inputs):
    import numpy as np
    import concourse.bacc as bacc
    from concourse.bass_utils import run_bass_kernel_spmd

    nc = bacc.Bacc("TRN2", target_bir_lowering=False, num_devices=1)
    arrays, args = {}, []
    for name in _INS:
        a = np.ascontiguousarray(inputs[name])
        if name in ("x", "w_in", "conv_w", "w_att_o", "w_conv_o", "w_out"):
            a = a.reshape(a.shape[1:])
        arrays[f"in_{name}"] = a
        args.append(nc.dram_tensor(f"in_{name}", a.shape, mybir.dt.from_np(a.dtype), kind="ExternalInput").ap())
    neg_c_dram = nc.dram_tensor("neg_c_dram", (HEADS, TOK), F32, kind="Internal").ap()
    out = nc.dram_tensor("out", (SEQ, D), F32, kind="ExternalOutput").ap()
    hybrid_block(nc, *args, neg_c_dram, out)
    r = run_bass_kernel_spmd(nc, [arrays], core_ids=[0])
    return r.results[0]["out"].reshape(1, SEQ, D)
```
